# Optimizing a Trainium2 kernel written in Bass

```python
import jax, jax.numpy as jnp
from jax import lax
import numpy as np

D_MODEL = 1024
BATCH = 1
SEQ = 512
DEPTH = 1

EPS = 1e-6
MLA_HEADS = 8
MLA_Q_LORA = 256
MLA_KV_LORA = 256
MLA_NOPE = 64
MLA_ROPE = 32
MLA_V = 64
MLA_QK = MLA_NOPE + MLA_ROPE
MLA_W = MLA_HEADS * MLA_V
ROPE_THETA = 10000.0
Q_BLOCK = 128
DN_HEADS = 8
DN_DK = 64
DN_DV = 64
DN_KW = DN_HEADS * DN_DK
DN_VW = DN_HEADS * DN_DV
DN_CONV = 5
DN_CHUNK = 64
MEM_TOKENS = 256
MEM_HEADS = 4
MEM_HD = 128
MEM_W = MEM_HEADS * MEM_HD
N_BRANCH = 3
D_FF = -(-8 * D_MODEL // (3 * 256)) * 256
IN_SIZES = (MLA_Q_LORA, MLA_KV_LORA, MLA_ROPE,
            DN_KW, DN_KW, DN_VW, DN_VW,
            2 * DN_HEADS, 2 * DN_HEADS,
            MEM_W,
            N_BRANCH * D_MODEL)
IN_COLS = sum(IN_SIZES)

kernel_name = "hybrid_mla_gdn_mem_encoder"

def split_last(t, sizes):
    out, off = [], 0
    for s in sizes:
        out.append(t[..., off:off + s])
        off += s
    return out

def rmsnorm(x, w):
    xf = x.astype(jnp.float32)
    y = xf * lax.rsqrt(jnp.mean(xf * xf, axis=-1, keepdims=True) + EPS)
    return (y * w.astype(jnp.float32)).astype(x.dtype)

def l2norm(x):
    return x * lax.rsqrt(jnp.sum(x * x, axis=-1, keepdims=True) + EPS)

def rope_tables(positions):
    inv_freq = 1.0 / (ROPE_THETA ** (jnp.arange(0, MLA_ROPE, 2, dtype=jnp.float32) / MLA_ROPE))
    ang = positions.astype(jnp.float32)[..., None] * inv_freq
    return jnp.cos(ang), jnp.sin(ang)

def apply_rope(x, cos, sin):
    xf = x.astype(jnp.float32)
    x1, x2 = xf[..., : MLA_ROPE // 2], xf[..., MLA_ROPE // 2:]
    return jnp.concatenate([x1 * cos - x2 * sin, x1 * sin + x2 * cos], axis=-1).astype(x.dtype)

def mla_branch(c_q, c_kv, k_rope_raw, cos, sin, q_norm, w_uq, kv_norm, w_ukv):
    B, S, _ = c_q.shape
    q = (rmsnorm(c_q, q_norm) @ w_uq).reshape(B, S, MLA_HEADS, MLA_QK)
    q_nope = q[..., :MLA_NOPE]
    q_rope = apply_rope(q[..., MLA_NOPE:], cos[:, :, None, :], sin[:, :, None, :])
    kv = (rmsnorm(c_kv, kv_norm) @ w_ukv).reshape(B, S, MLA_HEADS, MLA_NOPE + MLA_V)
    k_nope, v = kv[..., :MLA_NOPE], kv[..., MLA_NOPE:]
    k_rope = apply_rope(k_rope_raw, cos, sin)
    scale = MLA_QK ** -0.5
    nb = S // Q_BLOCK
    qn_b = q_nope.reshape(B, nb, Q_BLOCK, MLA_HEADS, MLA_NOPE).swapaxes(0, 1)
    qr_b = q_rope.reshape(B, nb, Q_BLOCK, MLA_HEADS, MLA_ROPE).swapaxes(0, 1)

    def block(args):
        qn, qr = args
        s = (jnp.einsum('bqhd,bkhd->bhqk', qn, k_nope)
             + jnp.einsum('bqhr,bkr->bhqk', qr, k_rope))
        p = jax.nn.softmax(s.astype(jnp.float32) * scale, axis=-1).astype(v.dtype)
        return jnp.einsum('bhqk,bkhd->bqhd', p, v)

    o = lax.map(block, (qn_b, qr_b))
    return o.swapaxes(0, 1).reshape(B, S, MLA_W)

def short_conv(x, w):
    C = x.shape[-1]
    y = lax.conv_general_dilated(
        x, w[:, None, :].astype(x.dtype), window_strides=(1,),
        padding=[(DN_CONV // 2, DN_CONV // 2)],
        dimension_numbers=('NWC', 'WIO', 'NWC'), feature_group_count=C)
    return jax.nn.silu(y)

def chunk_gated_delta(q, k, v, g, beta):
    B, S, H, DK = q.shape
    DV = v.shape[-1]
    C = DN_CHUNK
    N = S // C
    to_c = lambda t: jnp.moveaxis(t.reshape((B, N, C, H) + t.shape[3:]), 3, 1)
    q, k, v, g, beta = to_c(q), to_c(k), to_c(v), to_c(g), to_c(beta)
    gc = jnp.cumsum(g, axis=-1)
    kb = k * beta[..., None]
    vb = v * beta[..., None]
    idx = jnp.arange(C)
    incl = idx[:, None] >= idx[None, :]
    strict = idx[:, None] > idx[None, :]
    decay = jnp.exp(jnp.where(incl, gc[..., :, None] - gc[..., None, :], -jnp.inf))
    L = jnp.where(strict, jnp.einsum('bhnid,bhnjd->bhnij', kb, k) * decay, 0.0)
    A = L + jnp.eye(C, dtype=jnp.float32)
    tri = lambda rhs: lax.linalg.triangular_solve(A, rhs, left_side=True, lower=True,
                                                  unit_diagonal=True)
    u = tri(vb)
    w = tri(kb * jnp.exp(gc)[..., None])
    attn = jnp.einsum('bhnid,bhnjd->bhnij', q, k) * decay

    def step(state, inp):
        q_i, k_i, u_i, w_i, gc_i, attn_i = inp
        v_new = u_i - jnp.einsum('bhcd,bhde->bhce', w_i, state)
        o = (jnp.einsum('bhcd,bhde->bhce', q_i * jnp.exp(gc_i)[..., None], state)
             + jnp.einsum('bhij,bhje->bhie', attn_i, v_new))
        g_last = gc_i[..., -1]
        k_dec = k_i * jnp.exp(g_last[..., None] - gc_i)[..., None]
        state = state * jnp.exp(g_last)[..., None, None] + jnp.einsum('bhcd,bhce->bhde', k_dec, v_new)
        return state, o

    xs = tuple(jnp.moveaxis(t, 2, 0) for t in (q, k, u, w, gc, attn))
    s0 = jnp.zeros((B, H, DK, DV), jnp.float32)
    _, o = lax.scan(step, s0, xs)
    return jnp.moveaxis(o, 0, 2).swapaxes(1, 3).reshape(B, S, H, DV)

def deltanet_branch(dq, dk, dv, dz, da, db, conv_w, a_log, dt_bias, out_norm):
    B, S, _ = dq.shape
    qkv = short_conv(jnp.concatenate([dq, dk, dv], axis=-1), conv_w)
    q, k, v = split_last(qkv, (DN_KW, DN_KW, DN_VW))
    q = l2norm(q.reshape(B, S, DN_HEADS, DN_DK).astype(jnp.float32)) * (DN_DK ** -0.5)
    k = l2norm(k.reshape(B, S, DN_HEADS, DN_DK).astype(jnp.float32))
    v = v.reshape(B, S, DN_HEADS, DN_DV).astype(jnp.float32)
    a = da.reshape(B, S, 2, DN_HEADS).astype(jnp.float32)
    b = db.reshape(B, S, 2, DN_HEADS).astype(jnp.float32)
    g = -jnp.exp(a_log.astype(jnp.float32)) * jax.nn.softplus(a + dt_bias.astype(jnp.float32))
    beta = jax.nn.sigmoid(b)
    o_f = chunk_gated_delta(q, k, v, g[:, :, 0], beta[:, :, 0])
    rev = lambda t: jnp.flip(t, axis=1)
    o_b = rev(chunk_gated_delta(rev(q), rev(k), rev(v), rev(g[:, :, 1]), rev(beta[:, :, 1])))
    o = o_f + o_b
    z = dz.reshape(B, S, DN_HEADS, DN_DV).astype(jnp.float32)
    o = (o * lax.rsqrt(jnp.mean(o * o, axis=-1, keepdims=True) + EPS)
         * out_norm.astype(jnp.float32) * jax.nn.silu(z))
    return o.reshape(B, S, DN_VW).astype(dq.dtype)

def mem_branch(mq, mem, mem_norm_w, w_kv):
    B, S, _ = mq.shape
    kv = rmsnorm(mem, mem_norm_w) @ w_kv
    k = kv[..., :MEM_W].reshape(B, -1, MEM_HEADS, MEM_HD)
    v = kv[..., MEM_W:].reshape(B, -1, MEM_HEADS, MEM_HD)
    q = mq.reshape(B, S, MEM_HEADS, MEM_HD)
    s = jnp.einsum('bshd,bmhd->bhsm', q, k).astype(jnp.float32) * (MEM_HD ** -0.5)
    p = jax.nn.softmax(s, axis=-1).astype(v.dtype)
    return jnp.einsum('bhsm,bmhd->bshd', p, v).reshape(B, S, MEM_W)

def setup_inputs(seed: int = 0) -> dict:
    key = jax.random.key(seed)
    ks = iter(jax.random.split(key, 40))
    f32 = jnp.float32
    nrm = lambda shape, fan_in: jax.random.normal(next(ks), shape, f32) * (fan_in ** -0.5)
    gain = lambda shape: 1.0 + 0.02 * jax.random.normal(next(ks), shape, f32)
    L = DEPTH
    x = jax.random.normal(next(ks), (BATCH, SEQ, D_MODEL), f32)
    mem = jax.random.normal(next(ks), (BATCH, MEM_TOKENS, D_MODEL), f32)
    positions = (jnp.arange(SEQ, dtype=jnp.int32)[None, :]
                 + jax.random.randint(next(ks), (BATCH, 1), 0, 4096, dtype=jnp.int32))
    a_log = jnp.log(jax.random.uniform(next(ks), (L, 2, DN_HEADS), f32, 1.0, 16.0))
    dt = jnp.exp(jax.random.uniform(next(ks), (L, 2, DN_HEADS), f32,
                                    float(np.log(1e-3)), float(np.log(1e-1))))
    dt_bias = dt + jnp.log(-jnp.expm1(-dt))
    return {
        "x": x,
        "mem": mem,
        "positions": positions,
        "norm_mix": gain((L, D_MODEL)),
        "w_in": nrm((L, D_MODEL, IN_COLS), D_MODEL),
        "mla_q_norm": gain((L, MLA_Q_LORA)),
        "mla_w_uq": nrm((L, MLA_Q_LORA, MLA_HEADS * MLA_QK), MLA_Q_LORA),
        "mla_kv_norm": gain((L, MLA_KV_LORA)),
        "mla_w_ukv": nrm((L, MLA_KV_LORA, MLA_HEADS * (MLA_NOPE + MLA_V)), MLA_KV_LORA),
        "dn_conv": nrm((L, DN_CONV, 2 * DN_KW + DN_VW), DN_CONV),
        "dn_a_log": a_log,
        "dn_dt_bias": dt_bias,
        "dn_out_norm": gain((L, DN_DV)),
        "mem_norm": gain((L, D_MODEL)),
        "mem_w_kv": nrm((L, D_MODEL, 2 * MEM_W), D_MODEL),
        "w_branch_mla": nrm((L, MLA_W, D_MODEL), MLA_W),
        "w_branch_dn": nrm((L, DN_VW, D_MODEL), DN_VW),
        "w_branch_mem": nrm((L, MEM_W, D_MODEL), MEM_W),
        "w_out": nrm((L, D_MODEL, D_MODEL), D_MODEL),
        "norm_ffn": gain((L, D_MODEL)),
        "ffn_w_gate_up": nrm((L, D_MODEL, 2 * D_FF), D_MODEL),
        "ffn_w_down": nrm((L, D_FF, D_MODEL), D_FF),
        "final_norm": gain((D_MODEL,)),
    }

def reference(x, mem, positions, norm_mix, w_in, mla_q_norm, mla_w_uq, mla_kv_norm, mla_w_ukv,
              dn_conv, dn_a_log, dn_dt_bias, dn_out_norm, mem_norm, mem_w_kv,
              w_branch_mla, w_branch_dn, w_branch_mem, w_out, norm_ffn,
              ffn_w_gate_up, ffn_w_down, final_norm):
    B, S, D = x.shape
    cos, sin = rope_tables(positions)
    for l in range(DEPTH):
        h = rmsnorm(x, norm_mix[l])
        proj = h @ w_in[l]
        (c_q, c_kv, k_rope_raw, dq, dk, dv, dz, da, db, mq,
         gate_logits) = split_last(proj, IN_SIZES)
        o_mla = mla_branch(c_q, c_kv, k_rope_raw, cos, sin,
                           mla_q_norm[l], mla_w_uq[l], mla_kv_norm[l], mla_w_ukv[l])
        o_dn = deltanet_branch(dq, dk, dv, dz, da, db, dn_conv[l], dn_a_log[l],
                               dn_dt_bias[l], dn_out_norm[l])
        o_mem = mem_branch(mq, mem, mem_norm[l], mem_w_kv[l])
        gates = jax.nn.sigmoid(gate_logits.astype(jnp.float32)).astype(x.dtype)
        gates = gates.reshape(B, S, N_BRANCH, D)
        merged = (gates[:, :, 0] * (o_mla @ w_branch_mla[l])
                  + gates[:, :, 1] * (o_dn @ w_branch_dn[l])
                  + gates[:, :, 2] * (o_mem @ w_branch_mem[l]))
        x = x + merged @ w_out[l]
        h = rmsnorm(x, norm_ffn[l])
        gu = h @ ffn_w_gate_up[l]
        x = x + (jax.nn.silu(gu[..., :D_FF]) * gu[..., D_FF:]) @ ffn_w_down[l]
    return rmsnorm(x, final_norm)


_drawn_inputs = setup_inputs


def setup_inputs(seed=0):
    import zlib

    import numpy as np

    out = dict(_drawn_inputs(seed))
    spreads = {}
    factors = {'norm_mix': 4.131,
     'mla_q_norm': 21.451,
     'mla_kv_norm': 23.465,
     'dn_out_norm': 24.93,
     'mem_norm': 29.369,
     'norm_ffn': 13.97,
     'final_norm': 22.575}
    for name, (base, spread) in spreads.items():
        noise = np.random.default_rng([zlib.crc32(name.encode()), seed]).standard_normal(out[name].shape)
        drawn = base * np.exp(spread * noise) if base else spread * noise
        out[name] = __import__('jax').numpy.asarray(drawn.astype(out[name].dtype))
    for name, factor in factors.items():
        out[name] = (out[name] * factor).astype(out[name].dtype)
    return out
```

```python
from contextlib import ExitStack

import concourse.bass as bass
from concourse import mybir
import numpy as np

F32 = mybir.dt.float32
F32R = mybir.dt.float32r
BF16 = mybir.dt.bfloat16
I32 = mybir.dt.int32
ALU = mybir.AluOpType
ACT = mybir.ActivationFunctionType
AX = mybir.AxisListType

P = 128
SEQ, D = 512, 1024
NT, KD = SEQ // P, D // P
MEM = 256
NM = MEM // P
EPS = 1e-6
H, NOPE, ROPE, DV = 8, 64, 32, 64
QK = NOPE + ROPE
LORA = 256
MH, MHD = 4, 128
DK = 64
TAPS = 5
CT = 12
D_FF = 2816
NF = D_FF // P
LEVELS = 7
CHUNKS = SEQ // 64
NEG = -1e30
TWO_PI = 2 * np.pi
PI_A = 6.28125
PI_B = float(np.float32(round((TWO_PI - PI_A) * 2 ** 19) / 2 ** 19))
PI_C = float(np.float32(TWO_PI - PI_A - PI_B))
FAR = 4096.0
MAGIC = 1.5 * 2 ** 23

C_Q, C_KV, C_KR, C_DN, C_Z, C_AB, C_MQ, C_GATE = 0, 256, 512, 544, 2080, 2592, 2624, 3136
V_MIX, V_MEM, V_FFN, V_Q, V_KV, V_CONV = 0, 8, 16, 24, 26, 28
NV = V_CONV + TAPS * CT


def shape_tables():
    i = np.arange(P)
    row, col = i[:, None], i[None, :]
    parts = [np.eye(P), row <= col, row >= col, np.ones((P, P)),
             np.where(col >= row, 0.0, NEG), np.where(col <= row, 0.0, NEG)]
    for s in range(LEVELS):
        low = ((row >> (s + 1)) == (col >> (s + 1))) & ((row >> s) % 2 == 1) & ((col >> s) % 2 == 0)
        parts += [low | (row == col), low.T | (row == col)]
    freq = 1.0 / (np.float32(10000.0) ** (np.arange(0, ROPE, 2, dtype=np.float32) / np.float32(ROPE)))
    parts.append(np.broadcast_to(freq.astype(np.float32), (P, ROPE // 2)))
    return np.ascontiguousarray(np.concatenate([np.asarray(p, np.float32) for p in parts], axis=1))


def weight_blocks(w_in, w_uq, w_ukv, w_mem, w_br, w_out, w_gu, w_dn):
    def rows(w, c0, n, k0=0, k=KD):
        return w[k0 * P:(k0 + k) * P, c0:c0 + n].rearrange("(k p) n -> p k n", p=P)
    out = []
    for i in range(6):
        out.append((("dn", i), [rows(w_in, C_DN + 256 * i, 256)], KD, 256))
    out.append((("c", 0), [rows(w_in, C_Q, 256)], KD, 256))
    out.append((("c", 1), [rows(w_in, C_KV, 256)], KD, 256))
    out.append((("c", 2), [rows(w_in, C_KR, 32), rows(w_in, C_AB, 224)], KD, 256))
    for i in range(2):
        out.append((("mq", i), [rows(w_in, C_MQ + 256 * i, 256)], KD, 256))
    for i in range(4):
        out.append((("mkv", i), [rows(w_mem, 256 * i, 256)], KD, 256))
    out.append((("uq", 0), [rows(w_uq, 0, H * QK, k=2)], 2, H * QK))
    out.append((("ukv", 0), [rows(w_ukv, 0, H * 128, k=2)], 2, H * 128))
    for i in range(2):
        out.append((("z", i), [rows(w_in, C_Z + 256 * i, 256)], KD, 256))
    for c in range(4):
        for b in range(3):
            out.append((("gate", c, b), [rows(w_in, C_GATE + b * D + 256 * c, 256)], KD, 256))
        for b in range(3):
            out.append((("br", c, b), [rows(w_br[b], 256 * c, 256, k=4)], 4, 256))
    for half in range(2):
        for kk in range(2):
            out.append((("wo", half, kk), [rows(w_out, 512 * half, 512, 4 * kk, 4)], 4, 512))
    for f in range(NF):
        out.append((("gu", f), [rows(w_gu, f * P, P), rows(w_gu, D_FF + f * P, P)], KD, 256))
    for half in range(2):
        for f in range(0, NF, 4):
            n = min(4, NF - f)
            out.append((("down", half, f), [rows(w_dn, 512 * half, 512, f, n)], n, 512))
    return out


def psum_uses():
    uses, count, ring = {}, [0] * 8, {}

    def use(key, bank):
        uses[key] = (bank, count[bank])
        count[bank] += 1

    def turn(key, banks):
        n = ring.get(banks, 0)
        ring[banks] = n + 1
        use(key, banks[n % len(banks)])

    low, high, every = (0, 1, 2, 3), (4, 5, 6, 7), tuple(range(8))
    turn(("vec",), high)
    for k in range(KD):
        turn(("hT", k), every)
    for ct in range(CT):
        turn(("dn", ct), low)
    for cb in range(3):
        for t in range(NT):
            turn(("c", cb, t), low)
    for k in range(4):
        turn(("cT", k), high)
    for h in range(MH):
        turn(("mq", h), low)
    for k in range(KD):
        turn(("memT", k), high)
    turn(("gc",), high)
    turn(("gtot",), high)
    for h in range(MH):
        turn(("mk", h), low)
    for i in range(2):
        for m in range(NM):
            turn(("mv", i, m), low)

    def attention(name, heads):
        for n in range(NT * heads):
            turn((name, "S", n), (0, 1, 2))
        for n in range(NT * heads):
            turn((name, "PT", n), (4, 5))
        for t in range(NT):
            turn((name, "O", t), (6, 7))
            turn((name, "oT", t), (3,))
    attention("mem", MH)
    for t in range(NT):
        turn(("uqA", t), low)
        turn(("uqB", t), low)
        for g in range(2):
            turn(("qT", t, g), high)
    for t in range(NT):
        turn(("kvA", t), low)
        turn(("kvB", t), low)
        for g in range(2):
            turn(("kT", t, g), high)
    attention("mla", H)
    for k in range(4):
        turn(("z", k), low)
    for t in range(NT):
        for part in range(3):
            turn(("tok", t, part), high)
    turn(("rows",), high)
    for k in range(8):
        turn(("qkT", k), high)
    for g in range(NT + 1):
        if g < NT:
            for d in range(2):
                turn(("kb", g, d), low)
                for p in range(2):
                    turn(("D", g, d, p), low)
                for p in range(2):
                    turn(("G", g, d, p), low)
                    turn(("A", g, d, p), low)
            for b in range(4):
                turn(("X1", g, b), low)
            for s in range(1, LEVELS):
                for b in range(4):
                    turn(("P1", g, s, b), low)
                for kind in ("P3", "P2") if s < LEVELS - 1 else ("P3",):
                    for b in range(4):
                        turn((kind, g, s, b), low)
        if g > 0:
            for step in range(4):
                for d in range(2):
                    if step == 0 and g > 1:
                        turn(("kg", g - 1, d), high)
                        turn(("qg", g - 1, d), high)
                    if step == 1 and g > 1:
                        turn(("KS", g - 1, d), high)
                    if step == 2:
                        turn(("V", g - 1, d), high)
                    if step == 3:
                        turn(("O", g - 1, d), high)
                        if g < NT:
                            turn(("KV", g - 1, d), high)
    for k in range(4):
        turn(("odnT", k), high)
    for c in range(4):
        for kind in ("gate", "br"):
            for b in range(3):
                for j in range(2):
                    turn((kind, c, b, j), every)
    for half in range(2):
        for t in range(NT):
            use(("wo", half, t), 4 * half + t)
    for k in range(KD):
        turn(("h2T", k), every)
    for f in range(NF):
        turn(("g", f), every)
        turn(("u", f), every)
    for half in range(2):
        for t in range(NT):
            use(("down", half, t), 4 * half + t)
    return uses


def hybrid_encoder_kernel(nc, tables, x, mem, positions, norm_mix, w_in, mla_q_norm, mla_w_uq, mla_kv_norm,
                          mla_w_ukv, dn_conv, dn_a_log, dn_dt_bias, dn_out_norm, mem_norm, mem_w_kv,
                          w_branch_mla, w_branch_dn, w_branch_mem, w_out, norm_ffn, ffn_w_gate_up,
                          ffn_w_down, final_norm, out):
    blocks = weight_blocks(w_in[0], mla_w_uq[0], mla_w_ukv[0], mem_w_kv[0],
                           [w_branch_mla[0], w_branch_dn[0], w_branch_mem[0]], w_out[0],
                           ffn_w_gate_up[0], ffn_w_down[0])
    index = {b[0]: n for n, b in enumerate(blocks)}
    uses = psum_uses()
    in_sum = [b[0][0] == "wo" and b[0][2] == 0 or b[0][0] == "down" and b[0][2] + 4 < NF for b in blocks]
    parts_before = [sum(in_sum[:n]) for n in range(len(blocks))]
    FIRST_AFTER_DN = index[("gate", 0, 0)]
    RAW = 3

    ctx = ExitStack()
    with ctx:
        ctx.enter_context(nc.allow_non_contiguous_dma(reason="positions and small vectors, loaded once"))

        base = (nc.sbuf_base + 31) // 32 * 32
        top = [base]

        def at(name, shape, dt, offset):
            return nc.alloc_sbuf_tensor_at(name, shape, dt, offset=offset)

        def put(name, shape, dt=F32):
            size = int(np.prod(shape[1:])) * (2 if dt == BF16 else 4)
            t = at(name, shape, dt, top[0])
            top[0] += (size + 31) // 32 * 32
            return t

        KB = 1024
        ident = put("ident", [P, P])
        ident_b = put("ident_b", [P, P], BF16)
        neg_b = put("neg_b", [P, 2, P], BF16)
        shared = top[0]
        masks = put("masks", [P, 2 * LEVELS, P], BF16)
        upto = put("upto", [P, 2, P])
        gate_act = at("gate_act", [P, 2, SEQ], F32, shared)
        ones = put("ones", [P, P])
        freq = put("freq", [P, ROPE // 2])
        vcol = put("vcol", [P, NV])
        pos_i = put("pos_i", [P, NT], I32)
        pos_f = put("pos_f", [P, NT])
        cos = put("cos", [P, NT, ROPE // 2])
        sin = put("sin", [P, NT, ROPE // 2])
        krab = put("krab", [P, NT, 64])
        warm = put("warm", [P, 8])
        rope_k = put("rope_k", [P, 4, NT * ROPE // 2])
        small = put("small", [P, 4, 64])
        rstd = put("rstd", [P, 64])
        alog = put("alog", [P, 16])
        dtb = put("dtb", [P, 16])
        onorm = put("onorm", [P, 1])
        smax = put("smax", [P, 4])
        ssum = put("ssum", [P, 2, H])
        rinv = put("rinv", [P, 2, H])
        dg = put("dg", [P, 6, 64])
        egl = put("egl", [P, 64])
        edec = put("edec", [P, 64])

        ring = top[0]
        w_raw = [at(f"w_raw{i}", [P, 2048], F32, ring + 8 * KB * i) for i in range(RAW)]
        w_hi = [at(f"w_hi{i}", [P, 2048], F32R, ring + 8 * KB * (RAW + i)) for i in range(2)]
        w_lo = [at(f"w_lo{i}", [P, 2048], F32R, ring + 8 * KB * (RAW + 2 + i)) for i in range(2)]
        hbase = ring + 8 * KB * (RAW + 4)
        hT_hi = at("hT_hi", [P, KD, SEQ], F32R, hbase)
        hT_lo = at("hT_lo", [P, KD, SEQ], F32R, hbase + 16 * KB)
        v0 = hbase + 32 * KB
        assert v0 + 106 * KB <= nc.sbuf_usable_end, (v0 + 106 * KB, nc.sbuf_usable_end)

        def v(name, shape, kb, dt=F32):
            return at(name, shape, dt, v0 + int(kb * KB))

        dnT = v("dnT", [P, CT, SEQ], 0)
        zT = v("zT", [P, 4, SEQ], 24)
        oT_mla = v("oT_mla", [P, 4, SEQ], 32)
        oT_mem = v("oT_mem", [P, 4, SEQ], 40)
        x_tok = v("x_tok", [P, NT, D], 56)
        square = v("square", [P, D], 92)
        table_in = v("table_in", [P, 2 * LEVELS + 6, P], 80)
        vrow = v("vrow", [NV, P], 90)
        rope_t = v("rope_t", [P, 3, NT * ROPE // 2], 90.5)
        cT_hi = v("cT_hi", [P, 4, SEQ], 48, F32R)
        cT_lo = v("cT_lo", [P, 4, SEQ], 56, F32R)
        c_tok = v("c_tok", [P, NT, 512], 64)
        v_mla = v("v_mla", [P, NT, 512], 64)
        mqT = v("mqT", [P, MH, SEQ], 72)
        memT_hi = v("memT_hi", [P, KD, MEM], 80, F32R)
        memT_lo = v("memT_lo", [P, KD, MEM], 88, F32R)
        mem_tok = v("mem_tok", [P, NM, D], 96)
        mkT = v("mkT", [P, MH, MEM], 96)
        mv_tok = v("mv_tok", [P, NM, 512], 100)
        p_tok = v("p_tok", [P, 2, 512], 24)
        pT = v("pT", [P, 2, 512], 28)
        o_row = v("o_row", [P, 512], 104)
        qT = v("qT", [QK, H, SEQ], 72)
        kT = v("kT", [QK, H, SEQ], 88)
        qk_tok = v("qk_tok", [P, 2, H * QK], 24)
        rope_x = at("rope_x", [P, 4, 128], F32, v0 + 30 * KB)
        o_tok = v("o_tok", [P, NT, 512], 48)
        v_tok = v("v_tok", [P, NT, 512], 56)
        k_tok = v("k_tok", [P, NT, 512], 64)
        q_tok = v("q_tok", [P, NT, 512], 72)
        rows = [v(f"rows{i}", [64, NT, P], 16 + i, BF16) for i in range(3)]
        rows_rest = v("rows_rest", [64, NT, P], 88)
        pick = {1: v("pick1", [64, 2, 4, P], 104, BF16), 2: v("pick2", [64, 2, 4, P], 20, BF16),
                3: v("pick3", [64, 2, 4, P], 22, BF16)}
        square2 = v("square2", [P, 2, 512], 80)
        kbT = v("kbT", [P, 2, 4, P], 72)
        kgT = v("kgT", [P, 2, 4, P], 76)
        qgT = v("qgT", [P, 2, 4, P], 80)
        rowq = v("rowq", [P, NT, 64], 84)
        decT = v("decT", [P, 2, 4, P], 84)
        r_tok = v("r_tok", [P, 2, 512], 88)
        vdec = v("vdec", [P, 2, 512], 92)
        state = v("state", [P, 2, 4, P], 96)
        state_g = v("state_g", [P, 2, 4, P], 100)
        NTm = at("NTm", [P, 4, 4, P], F32, ring)
        X = at("X", [P, 4, 4, P], F32, ring + 8 * KB)
        T1 = at("T1", [P, 4, 4, P], F32, ring + 16 * KB)
        Z = [at(f"Z{i}", [P, 4, 4, P], F32, ring + (24 + 8 * i) * KB) for i in (1, 0)]
        attT = [at(f"attT{i}", [P, 4, 4, P], F32, ring + (40 + 8 * i) * KB) for i in (1, 0)]
        oT_dn = v("oT_dn", [P, 4, SEQ], 0)
        oT_hi = v("oT_hi", [P, 3, 4, SEQ], 56, F32R)
        oT_lo = v("oT_lo", [P, 3, 4, SEQ], 80, F32R)
        sig = v("sig", [P, 6, SEQ], 32)
        part = v("part", [P, 2, SEQ], 44)
        extra = v("extra", [P, 2, SEQ], 48)
        mT_hi = v("mT_hi", [P, KD, SEQ], 0, F32R)
        mT_lo = v("mT_lo", [P, KD, SEQ], 16, F32R)
        x1 = v("x1", [P, NT, D], 90)
        xs1 = v("xs1", [P, NT, D], 56)
        square3 = v("square3", [P, D], 72)
        act_hi = v("act_hi", [P, NF, SEQ], 0, F32R)
        act_lo = v("act_lo", [P, NF, SEQ], 2 * NF, F32R)
        fin_w = at("fin_w", [P, D], F32, hbase)
        y_out = at("y_out", [P, NT, D], F32, hbase + 4 * KB)
        square4 = at("square4", [P, D], F32, hbase + 20 * KB)

        psum = ctx.enter_context(nc.psum_tensor("psum", [P, 8, 512], F32))

        def sem(name):
            return ctx.enter_context(nc.semaphore(name))

        bank_full = [sem(f"bank_full{i}") for i in range(8)]
        bank_free = [sem(f"bank_free{i}") for i in range(8)]
        w_landed = [sem(f"w_landed{i}") for i in range(RAW)]
        w_hi_done, w_lo_done, w_part_used = sem("w_hi_done"), sem("w_lo_done"), sem("w_part_used")
        act_done, dve_done, pool_done = sem("act_done"), sem("dve_done"), sem("pool_done")
        x_landed = [sem(f"x_landed{t}") for t in range(NT)]
        consts_landed = sem("consts_landed")
        vec_landed = sem("vec_landed")
        mem_landed = sem("mem_landed")
        x1_landed = sem("x1_landed")
        fin_landed = sem("fin_landed")
        out_stored = sem("out_stored")
        consts_ready = sem("consts_ready")
        warm_ready = sem("warm_ready")
        rope_in = sem("rope_in")
        rope_ready = sem("rope_ready")
        ssq_ready = sem("ssq_ready")
        ms_ready = sem("ms_ready")
        root_ready = sem("root_ready")
        xs_ready = sem("xs_ready")
        split_hi = sem("split_hi")
        conv_first = sem("conv_first")
        dnT_ready = sem("dnT_ready")
        c_copied = sem("c_copied")
        max_ready = sem("max_ready")
        q_roped = sem("q_roped")
        qT_ready = sem("qT_ready")
        k_copied = sem("k_copied")
        k_placed = sem("k_placed")
        kT_ready = sem("kT_ready")
        kr_roped = sem("kr_roped")
        dg_x = sem("dg_x")
        dg_e = sem("dg_e")
        dg_g = sem("dg_g")
        gc_ready = sem("gc_ready")
        rowq_ready = sem("rowq_ready")
        tok_ready = sem("tok_ready")
        sq_ready = sem("sq_ready")
        qk_copied = sem("qk_copied")
        z1_ready = sem("z1_ready")
        vb_ready = sem("vb_ready")
        sg_ready = sem("sg_ready")
        vdec_ready = sem("vdec_ready")
        o_norm = sem("o_norm")
        rstd_dn = sem("rstd_dn")
        rows_hi_ready = sem("rows_hi_ready")
        rows_ready = sem("rows_ready")
        state_zero = sem("state_zero")
        merge_sum = sem("merge_sum")
        pv_done = sem("pv_done")
        osplit_hi = sem("osplit_hi")
        osplit_lo = sem("osplit_lo")
        merge_hi = sem("merge_hi")
        merge_lo = sem("merge_lo")
        glu_ready = sem("glu_ready")
        glu_hi = sem("glu_hi")
        x2_ready = sem("x2_ready")
        y_ready = sem("y_ready")
        o_squared = sem("o_squared")

        def bank(key, parts=P, cols=512):
            return psum[0:parts, uses[key][0], 0:cols]

        def claim(pe, key):
            b, n = uses[key]
            if n > 0:
                pe.wait_ge(bank_free[b], n)

        def filled(eng, key):
            b, n = uses[key]
            eng.wait_ge(bank_full[b], n + 1)

        def released(eng, key):
            b, n = uses[key]
            eng.wait_ge(bank_free[b], n + 1)

        def full(key):
            return bank_full[uses[key][0]]

        def free(key):
            return bank_free[uses[key][0]]

        def consumed(eng, n):
            kind, *i = blocks[n][0]
            last = {"dn": lambda: ("dn", 2 * i[0] + 1), "c": lambda: ("c", i[0], NT - 1), "mq": lambda: ("mq", 2 * i[0] + 1),
                    "mkv": lambda: ("mk", 2 * i[0] + 1) if i[0] < 2 else ("mv", i[0] - 2, NM - 1),
                    "uq": lambda: ("uqB", NT - 1), "ukv": lambda: ("kvB", NT - 1), "z": lambda: ("z", 2 * i[0] + 1),
                    "gate": lambda: ("gate", i[0], i[1], 1), "br": lambda: ("br", i[0], i[1], 1),
                    "wo": lambda: ("wo", i[0], NT - 1) if i[1] == 1 else None, "gu": lambda: ("u", i[0]),
                    "down": lambda: ("down", i[0], NT - 1) if i[1] + 4 >= NF else None}[kind]()
            if last:
                filled(eng, last)
            else:
                eng.wait_ge(w_part_used, parts_before[n] + 1)

        def wview(tiles, n):
            k, width = blocks[n][2], blocks[n][3]
            return tiles[n % len(tiles)][:, 0:k * width].rearrange("p (k n) -> p k n", k=k)

        def hi(name):
            return wview(w_hi, index[name])

        def lo(name):
            return wview(w_lo, index[name])

        def heads(ap, n=DK):
            return ap.unsqueeze(2).broadcast_to([P, ap.shape[1], n])

        def four(ap):
            return ap.unsqueeze(1).broadcast_to([P, 4, ap.shape[1]])

        def f32(ap):
            return ap.bitcast(F32)

        tile_of = lambda g, d: g if d == 0 else NT - 1 - g
        def col(t, d):
            return t * 16 + d * 8

        VEC_ROWS = [(norm_mix[0], V_MIX, 8), (mem_norm[0], V_MEM, 8), (norm_ffn[0], V_FFN, 8),
                    (mla_q_norm[0], V_Q, 2), (mla_kv_norm[0], V_KV, 2)]

        ROOTS_BEFORE = {"x": 0, "c": NT, "mem": NT + 1, "qk": NT + 2, "o": NT + 3, "ffn": NT + 4, "final": 2 * NT + 4}

        block = ctx.enter_context(nc.Block())

        @block.sync
        def _(sp):
            xt = x[0].rearrange("(t p) d -> t p d", p=P)
            sp.dma_start(ident[:, :], tables[:, 0:P]).then_inc(vec_landed, 16)
            for a, r, n in VEC_ROWS:
                sp.dma_start(vrow[r:r + n, :], a.rearrange("(r p) -> r p", p=P)).then_inc(vec_landed, 16)
            sp.dma_start(vrow[V_CONV:NV, :], dn_conv[0].rearrange("j (r p) -> (j r) p", p=P)).then_inc(vec_landed, 16)
            for t in range(NT):
                sp.dma_start(x_tok[:, t, :], xt[t]).then_inc(x_landed[t], 16)
            for n, (name, sources, k, width) in enumerate(blocks):
                if n == FIRST_AFTER_DN:
                    filled(sp, ("P1", NT - 1, LEVELS - 1, 3))
                if n == FIRST_AFTER_DN + 1:
                    filled(sp, ("P3", NT - 1, LEVELS - 1, 3))
                if n >= RAW:
                    sp.wait_ge(w_lo_done, n - RAW + 1)
                at_col = 0
                dst = w_raw[n % RAW][:, 0:k * width].rearrange("p (k n) -> p k n", k=k)
                for s in sources:
                    c = s.shape[2]
                    sp.dma_start(dst[:, :, at_col:at_col + c], s).then_inc(w_landed[n % RAW], 32 // len(sources))
                    at_col += c
            ot = out[0].rearrange("(t p) d -> t p d", p=P)
            for t in range(NT):
                sp.wait_ge(y_ready, t + 1)
                sp.dma_start(ot[t], y_out[:, t, :]).then_inc(out_stored, 16)
            sp.wait_ge(out_stored, 16 * NT)

        @block.gpsimd
        def _(pool):
            NC = 6 * P + 2 * LEVELS * P
            pool.memset(warm[:, 0:1], 1.0).then_inc(warm_ready, 1)
            pool.dma_start(table_in[:, :, :], tables[:, 0:NC].rearrange("p (a b) -> p a b", b=P)).then_inc(consts_landed, 16)
            pool.dma_start(upto[:, :, :], tables[:, P:3 * P].rearrange("p (a b) -> p a b", b=P)).then_inc(consts_landed, 16)
            pool.dma_start(ones[:, :], tables[:, 3 * P:4 * P]).then_inc(consts_landed, 16)
            pool.dma_start(freq[:, :], tables[:, NC:NC + ROPE // 2]).then_inc(consts_landed, 16)
            pool.dma_start(pos_i[:, :], positions[0].rearrange("(t p) -> p t", p=P)).then_inc(consts_landed, 16)
            pool.dma_start(alog[:, :], dn_a_log[0].rearrange("a b -> (a b)").partition_broadcast(P)).then_inc(consts_landed, 16)
            pool.dma_start(dtb[:, :], dn_dt_bias[0].rearrange("a b -> (a b)").partition_broadcast(P)).then_inc(consts_landed, 16)
            for u in range(2):
                pool.dma_start(onorm[u * DV:(u + 1) * DV, :],
                               dn_out_norm[0].rearrange("(p a) -> p a", a=1)).then_inc(consts_landed, 16)
            pool.dma_start(mem_tok[:, :, :], mem[0].rearrange("(t p) d -> p t d", p=P)).then_inc(mem_landed, 16)
            link_n = [0]

            def link(ins):
                link_n[0] += 1
                ins.then_inc(pool_done, 1)
                pool.wait_ge(pool_done, link_n[0])

            def rotate(xh, n, cb, sb, scratch, done, count):
                w = ROPE // 2
                t = [scratch[:, i, 0:n * w].rearrange("p (h w) -> p h w", w=w) for i in range(4)]
                lo_, hi_ = xh[:, :, 0:w], xh[:, :, w:2 * w]
                for dst, half, table in ((t[0], lo_, cb), (t[1], hi_, sb), (t[2], lo_, sb)):
                    link_n[0] += 1
                    pool.tensor_tensor(dst, half, table, ALU.mult).then_inc(pool_done, 1)
                link(pool.tensor_tensor(t[3], hi_, cb, ALU.mult))
                link(pool.tensor_tensor(lo_, t[0], t[1], ALU.subtract))
                pool.tensor_tensor(hi_, t[2], t[3], ALU.add).then_inc(done, 1)
                pool.wait_ge(done, count)

            pool.wait_ge(rope_ready, 2)
            released(pool, ("c", 2, NT - 1))
            rotate(krab[:, :, 0:ROPE], NT, cos[:, :, :], sin[:, :, :], rope_k, kr_roped, 1)
            released(pool, ("mem", "oT", NT - 1))
            for t in range(NT):
                released(pool, ("uqA", t))
                released(pool, ("uqB", t))
                qh = qk_tok[:, t % 2, :].rearrange("p (h n) -> p h n", n=QK)[:, :, NOPE:QK]
                cb, sb = (c[:, t, :].unsqueeze(1).broadcast_to([P, H, ROPE // 2]) for c in (cos, sin))
                rotate(qh, H, cb, sb, rope_x, q_roped, t + 1)

            pool.wait_ge(rstd_dn, 1)
            pool.wait_ge(qk_copied, 2 * NT)
            for t in range(NT):
                for q, buf in ((0, q_tok), (1, k_tok)):
                    bv = buf[:, t, :].rearrange("p (h n) -> p h n", n=DK)
                    sc = heads(rstd[:, q * 32 + t * 8:q * 32 + t * 8 + 8])
                    pool.tensor_tensor(bv, bv, sc, ALU.mult).then_inc(tok_ready, 1)

            for g in range(NT + 1):
                if g > 0:
                    for d in range(2):
                        t = tile_of(g - 1, d)
                        if g > 1:
                            filled(pool, ("O", g - 2, d))
                        rv = r_tok[:, d, :].rearrange("p (h n) -> p h n", n=DV)
                        beta = dg[:, 3, col(t, d):col(t, d) + 8]
                        pool.tensor_tensor(rv, v_tok[:, t, :].rearrange("p (h n) -> p h n", n=DV), heads(beta),
                                           ALU.mult).then_inc(vb_ready, 1)
                        if 1 < g < NT:
                            released(pool, ("KV", g - 2, d))
                            sv, gv = (b[:, d, :, :].rearrange("p j (u n) -> p (j u) n", u=2) for b in (state, state_g))
                            pool.tensor_tensor(gv, sv, heads(egl[:, col(t, d):col(t, d) + 8]),
                                               ALU.mult).then_inc(sg_ready, 1)
                if g == 0:
                    released(pool, ("qkT", 7))
                    pool.memset(state[:, :, :, :], 0.0).then_inc(state_zero, 1)
                if g < NT:
                    for b in range(4):
                        d = b // 2
                        released(pool, ("G", g, d, b % 2))
                        link(pool.affine_select(out=NTm[:, b, :, :], in_=NTm[:, b, :, :], compare_op=ALU.not_equal,
                                                fill=1.0, base=0, pattern=[[0, 4], [-1, P]], channel_multiplier=1))
                        pool.tensor_tensor(Z[g % 2][:, b, :, :], NTm[:, b, :, :], four(masks[:, 1 - d, :]),
                                           ALU.mult).then_inc(z1_ready, 1)
            consumed(pool, index[("br", 3, 2)])
            pool.dma_start(x1[:, :, :], x[0].rearrange("(t p) d -> p t d", p=P)).then_inc(x1_landed, 16)
            consumed(pool, index[("gu", NF - 1)])
            pool.dma_start(fin_w[:, :], final_norm.partition_broadcast(P)).then_inc(fin_landed, 16)

        @block.tensor
        def _(pe):
            def need(name):
                pe.wait_ge(w_lo_done, index[name] + 1)

            def product(o, s_hi, s_lo, m_hi, m_lo, first, last):
                pe.matmul(o, s_hi, m_hi, start=first, stop=False)
                pe.matmul(o, s_hi, m_lo, start=False, stop=False)
                return pe.matmul(o, s_lo, m_hi, start=False, stop=last)

            def by_feature(key, wname, c0, a_hi, a_lo, n=SEQ, k_n=KD, source=None):
                claim(pe, key)
                o = bank(key, P, n)
                wh, wl = hi(wname), lo(wname)
                for k in range(k_n):
                    if source:
                        released(pe, (source, k))
                    m = product(o, wh[:, k, c0:c0 + P], wl[:, k, c0:c0 + P], a_hi[:, k, 0:n], a_lo[:, k, 0:n],
                                k == 0, k == k_n - 1)
                m.then_inc(full(key), 1)

            def by_token(key, wname, c0, c1, a_hi, a_lo, t, k_n=KD, k0=0):
                claim(pe, key)
                o = bank(key, P, c1 - c0)
                wh, wl = hi(wname), lo(wname)
                for k in range(k_n):
                    m = product(o, a_hi[:, k0 + k, t * P:(t + 1) * P], a_lo[:, k0 + k, t * P:(t + 1) * P],
                                wh[:, k, c0:c1], wl[:, k, c0:c1], k == 0, k == k_n - 1)
                m.then_inc(full(key), 1)

            pe.wait_ge(vec_landed, 16 * 7)
            claim(pe, ("vec",))
            pe.transpose(bank(("vec",), P, NV), vrow[:, :], ident[0:NV, 0:NV]).then_inc(full(("vec",)), 1)
            for t in range(NT):
                pe.wait_ge(xs_ready, t + 1)
                for k in range(KD):
                    if t == 0:
                        claim(pe, ("hT", k))
                    m = pe.transpose(bank(("hT", k))[:, t * P:(t + 1) * P], x_tok[:, t, k * P:(k + 1) * P], ident[:, :])
                    if t == NT - 1:
                        m.then_inc(full(("hT", k)), 1)

            for i in range(6):
                need(("dn", i))
                for j in range(2):
                    by_feature(("dn", 2 * i + j), ("dn", i), j * P, hT_hi, hT_lo,
                                   source="hT" if (i, j) == (0, 0) else None)
            for cb in range(3):
                need(("c", cb))
                for t in range(NT):
                    by_token(("c", cb, t), ("c", cb), 0, 256, hT_hi, hT_lo, t)
            for i in range(2):
                need(("mq", i))
                for j in range(2):
                    by_feature(("mq", 2 * i + j), ("mq", i), j * P, hT_hi, hT_lo)
            pe.wait_ge(xs_ready, 2 * NT)
            for k in range(4):
                claim(pe, ("cT", k))
                for t in range(NT):
                    m = pe.transpose(bank(("cT", k))[:, t * P:(t + 1) * P], c_tok[:, t, k * P:(k + 1) * P], ident[:, :])
                m.then_inc(full(("cT", k)), 1)
            pe.wait_ge(xs_ready, 2 * NT + NM)
            for k in range(KD):
                claim(pe, ("memT", k))
                for t in range(NM):
                    m = pe.transpose(bank(("memT", k))[:, t * P:(t + 1) * P], mem_tok[:, t, k * P:(k + 1) * P], ident[:, :])
                m.then_inc(full(("memT", k)), 1)
            pe.wait_ge(consts_landed, 16 * 9)
            pe.wait_ge(dg_g, 1)
            key = ("gc",)
            claim(pe, key)
            for t in range(NT):
                for d in range(2):
                    c = col(t, d)
                    m = pe.matmul(bank(key)[:, c:c + 8], upto[:, d, :], dg[:, 2, c:c + 8], start=True, stop=True)
            m.then_inc(full(key), 1)
            key = ("gtot",)
            claim(pe, key)
            pe.matmul(bank(key, P, 64), ones[:, :], dg[:, 2, :], start=True, stop=True).then_inc(full(key), 1)
            for i in range(4):
                need(("mkv", i))
                if i == 0:
                    released(pe, ("cT", 3))
                    released(pe, ("memT", KD - 1))
                for j in range(2):
                    if i < 2:
                        by_feature(("mk", 2 * i + j), ("mkv", i), j * P, memT_hi, memT_lo, n=MEM)
                    else:
                        by_token(("mv", i - 2, j), ("mkv", i), 0, 256, memT_hi, memT_lo, j)

            def attention(name, nh, nk, q_of, k_of, v_of, width):
                total = NT * nh
                cols = nk * P

                def scores(n):
                    t, h = divmod(n, nh)
                    key = (name, "S", n)
                    claim(pe, key)
                    pe.matmul(bank(key, P, cols), q_of(h)[:, t * P:(t + 1) * P], k_of(h), start=True,
                              stop=True).then_inc(full(key), 1)

                def turn(n):
                    key = (name, "PT", n)
                    released(pe, (name, "S", n))
                    claim(pe, key)
                    for k in range(nk):
                        m = pe.transpose(bank(key)[:, k * P:(k + 1) * P], p_tok[:, n % 2, k * P:(k + 1) * P], ident[:, :])
                    m.then_inc(full(key), 1)

                def values(n):
                    t, h = divmod(n, nh)
                    key = (name, "O", t)
                    if h == 0:
                        claim(pe, key)
                    released(pe, (name, "PT", n))
                    for k in range(nk):
                        m = pe.matmul(bank(key)[:, h * width:(h + 1) * width], pT[:, n % 2, k * P:(k + 1) * P],
                                      v_of(k, h), start=(k == 0), stop=(k == nk - 1))
                    m.then_inc(full(key) if h == nh - 1 else pv_done, 1)

                def rows(t):
                    key = (name, "oT", t)
                    claim(pe, key)
                    released(pe, (name, "O", t))
                    for k in range(4):
                        m = pe.transpose(bank(key)[:, k * P:(k + 1) * P], o_row[:, k * P:(k + 1) * P], ident[:, :])
                    m.then_inc(full(key), 1)

                scores(0)
                scores(1)
                for n in range(total):
                    if n + 2 < total:
                        scores(n + 2)
                    turn(n)
                    if n > 0:
                        values(n - 1)
                    if n % nh == min(2, nh - 1) and n > nh:
                        rows(n // nh - 1)
                values(total - 1)
                rows(NT - 1)

            released(pe, ("mv", 1, NM - 1))
            attention("mem", MH, NM, lambda h: mqT[:, h, :], lambda h: mkT[:, h, :],
                      lambda k, h: mv_tok[:, k, h * MHD:(h + 1) * MHD], MHD)

            need(("uq", 0))

            def up_q(t):
                by_token(("uqA", t), ("uq", 0), 0, 512, cT_hi, cT_lo, t, k_n=2)
                by_token(("uqB", t), ("uq", 0), 512, 768, cT_hi, cT_lo, t, k_n=2)

            def up_kv(t):
                by_token(("kvA", t), ("ukv", 0), 0, 512, cT_hi, cT_lo, t, k_n=2, k0=2)
                by_token(("kvB", t), ("ukv", 0), 512, 1024, cT_hi, cT_lo, t, k_n=2, k0=2)

            def head_T(which, t, ready):
                pe.wait_ge(ready, t + 1)
                for g in range(2):
                    key = (which, t, g)
                    claim(pe, key)
                    for j in range(4):
                        h = 4 * g + j
                        m = pe.transpose(bank(key, QK)[:, j * P:(j + 1) * P], qk_tok[:, t % 2, h * QK:(h + 1) * QK],
                                         ident[:, :])
                    m.then_inc(full(key), 1)

            for t in range(NT + 1):
                if t < NT:
                    up_q(t)
                if t > 0:
                    head_T("qT", t - 1, q_roped)
            need(("ukv", 0))
            for t in range(NT + 1):
                if t < NT:
                    up_kv(t)
                if t > 0:
                    head_T("kT", t - 1, k_placed)
            released(pe, ("qT", NT - 1, 1))
            released(pe, ("kT", NT - 1, 1))
            attention("mla", H, NT, lambda h: qT[:, h, :], lambda h: kT[:, h, :],
                      lambda k, h: v_mla[:, k, h * DV:(h + 1) * DV], DV)
            pe.wait_ge(dnT_ready, CT)
            for t in range(NT):
                for pt in range(3):
                    key = ("tok", t, pt)
                    claim(pe, key)
                    for j in range(4):
                        m = pe.transpose(bank(key)[:, j * P:(j + 1) * P], dnT[:, 4 * pt + j, t * P:(t + 1) * P], ident[:, :])
                    m.then_inc(full(key), 1)
            for i in range(2):
                need(("z", i))
                for j in range(2):
                    by_feature(("z", 2 * i + j), ("z", i), j * P, hT_hi, hT_lo)

            pe.wait_ge(rowq_ready, 1)
            key = ("rows",)
            claim(pe, key)
            for t in range(NT):
                m = pe.transpose(bank(key, 64)[:, t * P:(t + 1) * P], rowq[:, t, :], ident[:, :])
            m.then_inc(full(key), 1)
            pe.wait_ge(tok_ready, 2 * NT)
            for k in range(8):
                src = q_tok if k < 4 else k_tok
                key = ("qkT", k)
                claim(pe, key)
                for t in range(NT):
                    m = pe.transpose(bank(key)[:, t * P:(t + 1) * P], src[:, t, (k % 4) * P:(k % 4 + 1) * P], ident[:, :])
                m.then_inc(full(key), 1)

            def spread_pairs(key, quantity, t, d):
                claim(pe, key)
                for j in range(4):
                    for i in range(3):
                        m = pe.matmul(bank(key)[:, j * P:(j + 1) * P], pick[quantity][:, d, j, :], rows[i][:, t, :],
                                      start=(i == 0), stop=(i == 2))
                m.then_inc(full(key), 1)

            def prepare(g):
                for d in range(2):
                    t = tile_of(g, d)
                    spread_pairs(("kb", g, d), 1, t, d)
                    for p in range(2):
                        key = ("D", g, d, p)
                        claim(pe, key)
                        pe.matmul(bank(key), ident_b[:, :], four(neg_b[:, d, :]), start=True, stop=False,
                                  skip_group_check=True)
                        for j in range(4):
                            r = d * 8 + 2 * j + p
                            sel = ident_b[0:64, r:r + 1].broadcast_to([64, P])
                            for i in range(3):
                                m = pe.matmul(bank(key)[:, j * P:(j + 1) * P], sel, rows[i][:, t, :], start=False,
                                              stop=(j == 3 and i == 2), skip_group_check=True)
                        m.then_inc(full(key), 1)
                    released(pe, ("kb", g, d))
                    for p in range(2):
                        half = slice(64 * p, 64 * p + 64)
                        for which in ("G", "A"):
                            key = (which, g, d, p)
                            claim(pe, key)
                            for j in range(4):
                                lhs = dnT[half, 4 + j, t * P:(t + 1) * P]
                                rhs = kbT[half, d, j, :] if which == "G" else dnT[half, j, t * P:(t + 1) * P]
                                m = pe.matmul(bank(key)[:, j * P:(j + 1) * P], lhs, rhs, start=True, stop=True)
                            m.then_inc(full(key), 1)
                for b in range(4):
                    key = ("X1", g, b)
                    claim(pe, key)
                    pe.wait_ge(z1_ready, 4 * g + b + 1)
                    for j in range(4):
                        m = pe.transpose(bank(key)[:, j * P:(j + 1) * P], Z[g % 2][:, b, j, :], ident[:, :])
                    m.then_inc(full(key), 1)

            def level(g, s, half):
                zs = Z[g % 2]
                for b in range(4) if half == 0 else ():
                    key = ("P1", g, s, b)
                    claim(pe, key)
                    released(pe, ("P2", g, s - 1, b) if s > 1 else ("X1", g, b))
                    for j in range(4):
                        m = pe.matmul(bank(key)[:, j * P:(j + 1) * P], NTm[:, b, j, :], X[:, b, j, :], start=True, stop=True)
                    m.then_inc(full(key), 1)
                for b in range(4) if half == 1 else ():
                    released(pe, ("P1", g, s, b))
                    if s > 1:
                        released(pe, ("P3", g, s - 1, b))
                    key = ("P3", g, s, b)
                    claim(pe, key)
                    for j in range(4):
                        m = pe.matmul(bank(key)[:, j * P:(j + 1) * P], T1[:, b, j, :], zs[:, b, j, :], start=True, stop=True)
                    m.then_inc(full(key), 1)
                for b in range(4) if half == 1 and s < LEVELS - 1 else ():
                    released(pe, ("P3", g, s, b))
                    key = ("P2", g, s, b)
                    claim(pe, key)
                    for j in range(4):
                        m = pe.transpose(bank(key)[:, j * P:(j + 1) * P], zs[:, b, j, :], ident[:, :])
                    m.then_inc(full(key), 1)

            def scan(g, step):
                for d in range(2):
                    t = tile_of(g, d)
                    n = 2 * g + d
                    if step == 0 and g > 0:
                        spread_pairs(("kg", g, d), 2, t, d)
                        spread_pairs(("qg", g, d), 3, t, d)
                    if step == 1 and g > 0:
                        key = ("KS", g, d)
                        claim(pe, key)
                        released(pe, ("kg", g, d))
                        released(pe, ("KV", g - 1, d))
                        for j in range(4):
                            m = pe.matmul(bank(key)[:, j * P:(j + 1) * P], kgT[:, d, j, :], state[:, d, j, :],
                                          start=True, stop=True)
                        m.then_inc(full(key), 1)
                    if step == 2:
                        key = ("V", g, d)
                        claim(pe, key)
                        if g > 0:
                            released(pe, ("KS", g, d))
                        pe.wait_ge(vb_ready, n + 1)
                        for b in (2 * d, 2 * d + 1):
                            released(pe, ("P3", g, LEVELS - 1, b))
                        for h in range(H):
                            m = pe.matmul(bank(key)[:, h * DV:(h + 1) * DV], Z[g % 2][:, 2 * d + h % 2, h // 2, :],
                                          r_tok[:, d, h * DV:(h + 1) * DV], start=True, stop=True)
                        m.then_inc(full(key), 1)
                    if step == 3:
                        key = ("O", g, d)
                        claim(pe, key)
                        if g > 0:
                            released(pe, ("qg", g, d))
                            for j in range(4):
                                pe.matmul(bank(key)[:, j * P:(j + 1) * P], qgT[:, d, j, :], state[:, d, j, :],
                                          start=(j == 0), stop=False, skip_group_check=True)
                        released(pe, ("V", g, d))
                        for p in range(2):
                            released(pe, ("A", g, d, p))
                        for h in range(H):
                            m = pe.matmul(bank(key)[:, h * DV:(h + 1) * DV], attT[g % 2][:, 2 * d + h % 2, h // 2, :],
                                          r_tok[:, d, h * DV:(h + 1) * DV], start=(g == 0 and h == 0), stop=(h == H - 1),
                                          skip_group_check=True)
                        m.then_inc(full(key), 1)
                        if g < NT - 1:
                            key = ("KV", g, d)
                            claim(pe, key)
                            pe.wait_ge(vdec_ready, n + 1)
                            for j in range(4):
                                m = pe.matmul(bank(key)[:, j * P:(j + 1) * P], k_tok[:, t, j * P:(j + 1) * P],
                                              vdec[:, d, j * P:(j + 1) * P], start=True, stop=True)
                            m.then_inc(full(key), 1)

            def gate_tile(c, b, j):
                if j == 0:
                    need(("gate", c, b))
                by_feature(("gate", c, b, j), ("gate", c, b), j * P, hT_hi, hT_lo)

            released(pe, ("qkT", 7))
            pe.wait_ge(rows_ready, 4)
            pe.wait_ge(state_zero, 1)
            for g in range(NT + 1):
                if g < NT:
                    prepare(g)
                for s in range(1, LEVELS) if g < NT else ():
                    level(g, s, 0)
                    if g > 0 and s <= 4:
                        scan(g - 1, s - 1)
                    level(g, s, 1)
            scan(NT - 1, 0)
            scan(NT - 1, 1)
            gate_tile(0, 0, 0)
            scan(NT - 1, 2)
            gate_tile(0, 0, 1)
            scan(NT - 1, 3)
            gate_tile(0, 1, 0)
            gate_tile(0, 1, 1)
            pe.wait_ge(o_norm, 4)
            for k in range(4):
                key = ("odnT", k)
                claim(pe, key)
                for t in range(NT):
                    m = pe.transpose(bank(key)[:, t * P:(t + 1) * P], o_tok[:, t, k * P:(k + 1) * P], ident[:, :])
                m.then_inc(full(key), 1)

            for c in range(4):
                for b in range(3) if c > 0 else (2,):
                    for j in range(2):
                        gate_tile(c, b, j)
                if c == 0:
                    pe.wait_ge(osplit_lo, 3)
                for b in range(3):
                    need(("br", c, b))
                    for j in range(2):
                        by_feature(("br", c, b, j), ("br", c, b), j * P, oT_hi[:, b], oT_lo[:, b], k_n=4)
            for half in range(2):
                for kk in range(2):
                    if half == 0:
                        pe.wait_ge(merge_lo, 4 * (kk + 1))
                    need(("wo", half, kk))
                    wh, wl = hi(("wo", half, kk)), lo(("wo", half, kk))
                    for t in range(NT):
                        key = ("wo", half, t)
                        if kk == 0:
                            claim(pe, key)
                        for k in range(4):
                            kg = 4 * kk + k
                            m = product(bank(key), mT_hi[:, kg, t * P:(t + 1) * P], mT_lo[:, kg, t * P:(t + 1) * P],
                                        wh[:, k, :], wl[:, k, :], kg == 0, kg == KD - 1)
                        if kk == 1:
                            m.then_inc(full(key), 1)
                    if kk == 0:
                        m.then_inc(w_part_used, 1)

            def turn_x1(k, t):
                if t == 0:
                    claim(pe, ("h2T", k))
                m = pe.transpose(bank(("h2T", k))[:, t * P:(t + 1) * P], xs1[:, t, k * P:(k + 1) * P], ident[:, :])
                if t == NT - 1:
                    m.then_inc(full(("h2T", k)), 1)

            for t in range(NT):
                pe.wait_ge(xs_ready, 2 * NT + NM + t + 1)
                for k in range(KD // 2):
                    turn_x1(k, t)
            for k in range(KD // 2, KD):
                for t in range(NT):
                    turn_x1(k, t)
            for f in range(NF):
                need(("gu", f))
                by_feature(("g", f), ("gu", f), 0, hT_hi, hT_lo, source="h2T" if f == 0 else None)
                by_feature(("u", f), ("gu", f), P, hT_hi, hT_lo)
            for half in range(2):
                for f0 in range(0, NF, 4):
                    name = ("down", half, f0)
                    need(name)
                    if half == 0:
                        released(pe, ("u", min(f0 + 4, NF) - 1))
                    wh, wl = hi(name), lo(name)
                    for t in range(NT):
                        key = ("down", half, t)
                        if f0 == 0:
                            claim(pe, key)
                        for f in range(f0, min(f0 + 4, NF)):
                            m = product(bank(key), act_hi[:, f, t * P:(t + 1) * P], act_lo[:, f, t * P:(t + 1) * P],
                                        wh[:, f - f0, :], wl[:, f - f0, :], f == 0, f == NF - 1)
                        if f0 + 4 >= NF:
                            m.then_inc(full(key), 1)
                    if f0 + 4 < NF:
                        m.then_inc(w_part_used, 1)

        @block.scalar
        def _(act):
            link_n = [0]

            def link(ins):
                link_n[0] += 1
                ins.then_inc(act_done, 1)
                act.wait_ge(act_done, link_n[0])

            def A(o, i, f=ACT.Copy, **kw):
                return nc.scalar.activation(o, i, f, **kw)

            def prep(name):
                if name is None:
                    return
                n = index[name]
                act.wait_ge(w_landed[n % RAW], 32 * (n // RAW + 1))
                if n >= 2:
                    consumed(act, n - 2)
                size = blocks[n][2] * blocks[n][3]
                A(w_hi[n % 2][:, 0:size], w_raw[n % RAW][:, 0:size]).then_inc(w_hi_done, 1)

            def after(name):
                n = index[name] + 1
                return blocks[n][0] if n < len(blocks) and n != FIRST_AFTER_DN else None

            ssq_n = [0]

            def squares(src, scratch, dst):
                if ssq_n[0]:
                    act.wait_ge(ssq_ready, ssq_n[0])
                ssq_n[0] += 1
                A(scratch, src, ACT.Square, accum_out=dst).then_inc(ssq_ready, 1)

            def root(which, out_, in_, t=0):
                act.wait_ge(ms_ready, ROOTS_BEFORE[which] + t + 1)
                A(out_, in_, ACT.Sqrt).then_inc(root_ready, 1)

            warm_n = [0]

            def root_tables():
                warm_n[0] += 1
                A(warm[:, warm_n[0]:warm_n[0] + 1], warm[:, 0:1], ACT.Sqrt)

            def split_T(key, dst, vec, cols=SEQ):
                filled(act, key)
                A(dst, bank(key, P, cols), scale=vcol[:, vec:vec + 1]).then_inc(split_hi, 1)

            act.wait_ge(warm_ready, 1)
            root_tables()
            for t in range(NT):
                act.wait_ge(x_landed[t], 16)
                squares(x_tok[:, t, :], square[:, :], small[:, 0, t:t + 1])
                root("x", small[:, 2, t:t + 1], small[:, 1, t:t + 1], t)
            filled(act, ("vec",))
            ins = A(vcol[:, :], bank(("vec",), P, NV))
            ins.then_inc(free(("vec",)), 1)
            released(act, ("vec",))
            prep(("dn", 0))
            for k in range(KD):
                split_T(("hT", k), hT_hi[:, k, :], V_MIX + k)
            prep(("dn", 1))
            act.wait_ge(rope_in, 1)
            w = NT * ROPE // 2
            A(sin[:, :, :].rearrange("p t w -> p (t w)"), rope_t[:, 0, :], ACT.Sin).then_inc(rope_ready, 1)
            A(cos[:, :, :].rearrange("p t w -> p (t w)"), rope_t[:, 1, :], ACT.Sin).then_inc(rope_ready, 1)

            for i in range(6):
                if i > 0:
                    prep(after(("dn", i)))
                for j in range(2):
                    ct = 2 * i + j
                    filled(act, ("dn", ct))
                    c = V_CONV + 2 * CT + ct
                    A(dnT[:, ct, :], bank(("dn", ct)), scale=vcol[:, c:c + 1]).then_inc(conv_first, 1)
                    if ct > 0:
                        released(act, ("dn", ct - 1))
                        A(dnT[:, ct - 1, :], dnT[:, ct - 1, :], ACT.Silu).then_inc(dnT_ready, 1)
            for cb in range(3):
                prep(after(("c", cb)))
                for t in range(NT):
                    key = ("c", cb, t)
                    filled(act, key)
                    if cb < 2:
                        A(c_tok[:, t, 256 * cb:256 * cb + 256], bank(key, P, 256)).then_inc(c_copied, 1)
                        n = cb * NT + t
                        if n >= 4:
                            released(act, ("c", (n - 4) // NT, (n - 4) % NT))
                        ins = A(square[:, 256 * (n % 4):256 * (n % 4) + 256], bank(key, P, 256), ACT.Square,
                                accum_out=small[:, 0, cb * NT + t:cb * NT + t + 1])
                        ins.then_inc(free(key), 1)
                    else:
                        ins = A(krab[:, t, :], bank(key, P, 64))
                        ins.then_inc(free(key), 1)
                if cb == 0:
                    released(act, ("dn", CT - 1))
                    A(dnT[:, CT - 1, :], dnT[:, CT - 1, :], ACT.Silu).then_inc(dnT_ready, 1)
            prep(("mq", 1))
            root("c", small[:, 2, 0:2 * NT], small[:, 1, 0:2 * NT])
            act.wait_ge(mem_landed, 16)
            for t in range(NM):
                squares(mem_tok[:, t, :], square[:, :], small[:, 0, 32 + t:33 + t])
            root("mem", small[:, 2, 32:32 + NM], small[:, 1, 32:32 + NM])
            act.wait_ge(dg_x, 1)
            link(A(dg[:, 4, :], dg[:, 0, :], ACT.Abs))
            link(A(dg[:, 4, :], dg[:, 4, :], ACT.Exp, scale=-1.0))
            link(A(dg[:, 4, :], dg[:, 4, :], ACT.Ln, bias=1.0))
            link(A(alog[:, :], alog[:, :], ACT.Exp))
            A(dg[:, 3, :], dg[:, 1, :], ACT.Exp, scale=-1.0).then_inc(dg_e, 1)
            for i in range(2):
                if i == 1:
                    prep(after(("mq", i)))
                for j in range(2):
                    key = ("mq", 2 * i + j)
                    filled(act, key)
                    ins = A(mqT[:, 2 * i + j, :], bank(key))
                    ins.then_inc(free(key), 1)
            for k in range(4):
                split_T(("cT", k), cT_hi[:, k, :], V_Q + k)
            for k in range(KD):
                split_T(("memT", k), memT_hi[:, k, :], V_MEM + k, MEM)
            for i in range(4):
                prep(after(("mkv", i)))
                for j in range(2):
                    if i < 2:
                        key, dst, sc = ("mk", 2 * i + j), mkT[:, 2 * i + j, :], MHD ** -0.5
                    else:
                        key, dst, sc = ("mv", i - 2, j), mv_tok[:, j, 256 * (i - 2):256 * (i - 2) + 256], 1.0
                    filled(act, key)
                    ins = A(dst, bank(key, P, 256), scale=sc)
                    ins.then_inc(free(key), 1)

            def attention(name, nh, nk, base_n, dst):
                cols = nk * P
                for n in range(NT * nh):
                    t, h = divmod(n, nh)
                    key = (name, "S", n)
                    act.wait_ge(max_ready, base_n + n + 1)
                    if n >= 2:
                        filled(act, (name, "PT", n - 2))
                    if h == 0 and t >= 2:
                        released(act, (name, "O", t - 2))
                    ins = A(p_tok[:, n % 2, 0:cols], bank(key, P, cols), ACT.Exp, bias=smax[:, n % 4:n % 4 + 1],
                            accum_out=ssum[:, t % 2, h:h + 1])
                    ins.then_inc(free(key), 1)
                    if h == min(4, nh - 1) and t > 0:
                        out_T(name, t - 1, dst)
                out_T(name, NT - 1, dst)

            def out_T(name, t, dst):
                key = (name, "oT", t)
                filled(act, key)
                ins = A(dst[:, :, t * P:(t + 1) * P], bank(key).rearrange("p (k n) -> p k n", k=4))
                ins.then_inc(free(key), 1)

            act.wait_ge(gc_ready, 1)
            link(A(dg[:, 4, :], dg[:, 0, :], ACT.Exp))
            link(A(edec[:, :], dg[:, 5, :], ACT.Exp))
            A(egl[:, :], dg[:, 1, :], ACT.Exp).then_inc(gc_ready, 1)
            attention("mem", MH, NM, 0, oT_mem)
            prep(("ukv", 0))

            def heads_T(which, dst, t, ready):
                for g in range(2):
                    key = (which, t, g)
                    filled(act, key)
                    ins = A(dst[:, 4 * g:4 * g + 4, t * P:(t + 1) * P], bank(key, QK).rearrange("p (h n) -> p h n", h=4))
                    ins.then_inc(free(key), 1)

            for t in range(NT + 1):
                if t < NT:
                    if t >= 2:
                        filled(act, ("qT", t - 2, 1))
                    for key, c0, c1 in ((("uqA", t), 0, 512), (("uqB", t), 512, 768)):
                        filled(act, key)
                        ins = A(qk_tok[:, t % 2, c0:c1], bank(key, P, c1 - c0), scale=QK ** -0.5)
                        ins.then_inc(free(key), 1)
                if t > 0:
                    heads_T("qT", qT, t - 1, qT_ready)
            prep(("z", 0))
            for t in range(NT + 1):
                if t < NT:
                    for i, nm in enumerate(("kvA", "kvB")):
                        key = (nm, t)
                        filled(act, key)
                        kvh = bank(key).rearrange("p (h n) -> p h n", n=128)
                        A(v_mla[:, t, 256 * i:256 * i + 256].rearrange("p (h n) -> p h n", n=DV),
                          kvh[:, :, NOPE:128]).then_inc(k_copied, 1)
                if t > 0:
                    heads_T("kT", kT, t - 1, kT_ready)
            attention("mla", H, NT, NT * MH, oT_mla)
            for t in range(NT):
                for pt, buf in enumerate((q_tok, k_tok)):
                    key = ("tok", t, pt)
                    filled(act, key)
                    A(buf[:, t, :], bank(key)).then_inc(qk_copied, 1)
                    n = 2 * t + pt
                    if n >= 2:
                        act.wait_ge(sq_ready, n - 1)
                    ins = A(square2[:, n % 2, :], bank(key), ACT.Square)
                    ins.then_inc(free(key), 1)
            root("qk", small[:, 2, :], small[:, 1, :])
            for i in range(2):
                prep(after(("z", i)))
                for k in (2 * i, 2 * i + 1):
                    key = ("z", k)
                    filled(act, key)
                    ins = A(zT[:, k, :], bank(key), ACT.Silu)
                    ins.then_inc(free(key), 1)

            filled(act, ("rows",))
            A(rows[0][:, :, :], bank(("rows",), 64).rearrange("p (t n) -> p t n", t=NT)).then_inc(rows_hi_ready, 1)
            for k in range(8):
                key = ("qkT", k)
                filled(act, key)
                ins = A(dnT[:, k, :], bank(key))
                ins.then_inc(free(key), 1)

            def scan(g, step):
                for d in range(2):
                    n = 2 * g + d
                    if step == 2:
                        key = ("V", g, d)
                        if g < NT - 1:
                            act.wait_ge(vdec_ready, n + 1)
                        else:
                            filled(act, key)
                        ins = A(r_tok[:, d, :], bank(key))
                        ins.then_inc(free(key), 1)
                    if step == 3 and g < 2:
                        key = ("O", g, d)
                        filled(act, key)
                        A(o_tok[:, tile_of(g, d), :], bank(key)).then_inc(free(key), 1)

            for g in range(NT):
                if g < NT:
                    for d in range(2):
                        for p in range(2):
                            key = ("D", g, d, p)
                            filled(act, key)
                            n = 4 * g + 2 * d + p
                            if n >= 2:
                                released(act, ("A", (n - 2) // 4, (n - 2) // 2 % 2, p))
                            for j in range(4):
                                c = col(tile_of(g, d), d) + 2 * j + p
                                ins = A(decT[:, p, j, :], bank(key)[:, j * P:(j + 1) * P], ACT.Exp, bias=dg[:, 2, c:c + 1])
                            ins.then_inc(free(key), 1)
                    for b in range(4):
                        key = ("X1", g, b)
                        filled(act, key)
                        ins = A(X[:, b, :, :], bank(key).rearrange("p (h n) -> p h n", h=4))
                        ins.then_inc(free(key), 1)
                for s in range(1, LEVELS):
                    if g < NT:
                        for b in range(4):
                            key = ("P3", g, s, b)
                            filled(act, key)
                            ins = A(Z[g % 2][:, b, :, :], bank(key).rearrange("p (h n) -> p h n", h=4))
                            ins.then_inc(free(key), 1)
                        if g > 0 and s <= 4:
                            scan(g - 1, s - 1)
                        for b in range(4) if s < LEVELS - 1 else ():
                            key = ("P2", g, s, b)
                            filled(act, key)
                            ins = A(X[:, b, :, :], bank(key).rearrange("p (h n) -> p h n", h=4))
                            ins.then_inc(free(key), 1)
            for d in range(2):
                filled(act, ("O", NT - 2, d))
            prep(("gate", 0, 0))
            for step in range(4):
                scan(NT - 1, step)
            for d in range(2):
                filled(act, ("V", NT - 1, d))
            prep(("gate", 0, 1))
            prep(("gate", 0, 2))
            for d in range(2):
                released(act, ("O", NT - 2, d))
                released(act, ("O", NT - 1, d))
            root_tables()
            for t in range(NT):
                if t >= 2:
                    act.wait_ge(sq_ready, 2 * NT + t - 1)
                A(square2[:, t % 2, :], o_tok[:, t, :], ACT.Square).then_inc(o_squared, 1)
            root("o", small[:, 2, 0:32], small[:, 1, 0:32])
            act.wait_ge(vb_ready, 2 * NT)
            for b, src in ((0, oT_mla), (2, oT_mem)):
                A(oT_hi[:, b, :, :], src[:, :, :]).then_inc(osplit_hi, 1)
            for k in range(4):
                released(act, ("odnT", k))
            A(oT_hi[:, 1, :, :], oT_dn[:, :, :]).then_inc(osplit_hi, 1)
            act.wait_ge(osplit_lo, 2)
            for c in range(4):
                for b in range(3):
                    if c > 0 or b == 2:
                        prep(after(("gate", c, b)))
                    for j in range(2):
                        key = ("gate", c, b, j)
                        filled(act, key)
                        if c > 0:
                            released(act, ("br", c - 1, b, j))
                        ins = A(sig[:, 2 * b + j, :], bank(key), ACT.Sigmoid)
                        ins.then_inc(free(key), 1)
                for b in range(3):
                    prep(after(("br", c, b)))
                for j in range(2):
                    act.wait_ge(merge_sum, 2 * c + j + 1)
                    A(mT_hi[:, 2 * c + j, :], part[:, j, :]).then_inc(merge_hi, 1)
            for half in range(2):
                for kk in range(2):
                    prep(after(("wo", half, kk)))
            root_tables()
            for t in range(NT):
                released(act, ("wo", 1, t))
                squares(x1[:, t, :], square3[:, :], small[:, 0, t:t + 1])
                root("ffn", small[:, 2, t:t + 1], small[:, 1, t:t + 1], t)
            for k in range(KD):
                split_T(("h2T", k), hT_hi[:, k, :], V_FFN + k)
            for f in range(NF):
                prep(after(("gu", f)))
                filled(act, ("g", f))
                if f >= 2:
                    act.wait_ge(glu_ready, f - 1)
                ins = A(gate_act[:, f % 2, :], bank(("g", f)), ACT.Silu)
                ins.then_inc(free(("g", f)), 1)
                act.wait_ge(glu_ready, f + 1)
                A(act_hi[:, f, :], bank(("u", f))).then_inc(glu_hi, 1)
            for half in range(2):
                for f0 in range(0, NF, 4):
                    prep(after(("down", half, f0)))
            root_tables()
            for t in range(NT):
                act.wait_ge(x2_ready, NT + t + 1)
                squares(x1[:, t, :], square4[:, :], small[:, 0, t:t + 1])
                root("final", small[:, 2, t:t + 1], small[:, 1, t:t + 1], t)

        @block.vector
        def _(dve):
            link_n = [0]

            def link(ins):
                link_n[0] += 1
                ins.then_inc(dve_done, 1)
                dve.wait_ge(dve_done, link_n[0])

            def tt(o, a, b, op):
                return dve.tensor_tensor(o, a, b, op)

            def prep(name):
                if name is None:
                    return
                n = index[name]
                size = blocks[n][2] * blocks[n][3]
                dve.wait_ge(w_hi_done, n + 1)
                tt(w_lo[n % 2][:, 0:size], w_raw[n % RAW][:, 0:size], f32(w_hi[n % 2][:, 0:size]),
                   ALU.subtract).then_inc(w_lo_done, 1)

            def after(name):
                n = index[name] + 1
                return blocks[n][0] if n < len(blocks) and n != FIRST_AFTER_DN else None

            def rsqrt(which, cols, width, dst, t=0):
                ssq, ms, root, tmp = (small[:, i, cols] for i in range(4))
                ins = dve.tensor_scalar(ms, ssq, 1.0 / width, EPS, ALU.mult, ALU.add)
                ins.then_inc(ms_ready, 1)
                dve.wait_ge(root_ready, ROOTS_BEFORE[which] + t + 1)
                link(dve.reciprocal(root, root))
                link(tt(tmp, root, root, ALU.mult))
                link(tt(tmp, tmp, ms, ALU.mult))
                link(dve.tensor_scalar(tmp, tmp, -0.5, 1.5, ALU.mult, ALU.add))
                link(tt(dst, root, tmp, ALU.mult))

            def split_T(n, key, dst_hi, dst_lo, vec, cols=SEQ):
                dve.wait_ge(split_hi, n + 1)
                ins = dve.scalar_tensor_tensor(out=dst_lo, in0=bank(key, P, cols), scalar=vcol[:, vec:vec + 1],
                                               in1=f32(dst_hi), op0=ALU.mult, op1=ALU.subtract)
                ins.then_inc(free(key), 1)

            for t in range(NT):
                dve.wait_ge(ssq_ready, t + 1)
                rsqrt("x", slice(t, t + 1), D, rstd[:, t:t + 1], t)
                dve.tensor_scalar(x_tok[:, t, :], x_tok[:, t, :], rstd[:, t:t + 1], None, ALU.mult).then_inc(xs_ready, 1)
            released(dve, ("vec",))
            prep(("dn", 0))
            for k in range(KD):
                split_T(k, ("hT", k), hT_hi[:, k, :], hT_lo[:, k, :], V_MIX + k)
            prep(("dn", 1))
            dve.wait_ge(consts_landed, 16 * 9)
            dve.tensor_copy(ident_b[:, :], table_in[:, 0, :]).then_inc(consts_ready, 1)
            dve.tensor_copy(neg_b[:, :, :], table_in[:, 4:6, :]).then_inc(consts_ready, 1)
            dve.tensor_copy(masks[:, :, :], table_in[:, 6:6 + 2 * LEVELS, :]).then_inc(consts_ready, 1)
            link(dve.tensor_copy(pos_f[:, :], pos_i[:, :]))
            w = ROPE // 2
            ang, turns, half_turn = rope_t[:, 0, :], rope_t[:, 1, :], rope_t[:, 2, :]
            link(tt(ang.rearrange("p (t w) -> p t w", w=w), pos_f[:, :].unsqueeze(2).broadcast_to([P, NT, w]),
                    freq[:, :].unsqueeze(1).broadcast_to([P, NT, w]), ALU.mult))
            for far in (FAR, 1.0):
                link(dve.tensor_scalar(turns, ang, 1.0 / (TWO_PI * far), MAGIC, ALU.mult, ALU.add))
                link(dve.tensor_scalar(turns, turns, -MAGIC, None, ALU.add))
                for piece in (PI_A, PI_B, PI_C):
                    link(dve.scalar_tensor_tensor(out=ang, in0=turns, scalar=-piece * far, in1=ang,
                                                  op0=ALU.mult, op1=ALU.add))
            link(dve.tensor_scalar(turns, ang, np.pi / 2, None, ALU.add))
            link(dve.tensor_scalar(half_turn, turns, float(np.pi), -TWO_PI, ALU.is_gt, ALU.mult))
            link(tt(turns, turns, half_turn, ALU.add))
            link(dve.tensor_scalar(turns, turns, 3.1415925, -3.1415925, ALU.min, ALU.max))
            dve.tensor_scalar(ang, ang, 3.1415925, -3.1415925, ALU.min, ALU.max).then_inc(rope_in, 1)

            for i in range(6):
                if i > 0:
                    prep(after(("dn", i)))
                for j in range(2):
                    ct = 2 * i + j
                    key = ("dn", ct)
                    dve.wait_ge(conv_first, ct + 1)
                    for tap in (0, 1, 3, 4):
                        s = tap - TAPS // 2
                        a, b = max(0, -s), SEQ - max(0, s)
                        c = V_CONV + tap * CT + ct
                        ins = dve.scalar_tensor_tensor(out=dnT[:, ct, a:b], in0=bank(key)[:, a + s:b + s],
                                                       scalar=vcol[:, c:c + 1], in1=dnT[:, ct, a:b],
                                                       op0=ALU.mult, op1=ALU.add)
                        if tap < 4:
                            link(ins)
                    ins.then_inc(free(key), 1)
            for cb in range(3):
                prep(after(("c", cb)))
            prep(("mq", 1))
            released(dve, ("c", 2, NT - 1))
            ab = krab[:, :, :].rearrange("p t (u n) -> p t u n", u=4)
            view = lambda i: dg[:, i, :].rearrange("p (t n) -> p t n", t=NT)
            each = lambda s: s.unsqueeze(1).broadcast_to([P, NT, 16])
            link(tt(view(0), ab[:, :, 2, :], each(dtb[:, :]), ALU.add))
            dve.tensor_copy(view(1), ab[:, :, 3, :]).then_inc(dg_x, 1)
            rsqrt("c", slice(0, 2 * NT), LORA, rstd[:, 0:2 * NT])
            dve.wait_ge(c_copied, 2 * NT)
            for t in range(NT):
                dve.tensor_scalar(c_tok[:, t, 0:256], c_tok[:, t, 0:256], rstd[:, t:t + 1], None, ALU.mult)
                dve.tensor_scalar(c_tok[:, t, 256:512], c_tok[:, t, 256:512], rstd[:, NT + t:NT + t + 1], None,
                                  ALU.mult).then_inc(xs_ready, 1)
            dve.wait_ge(ssq_ready, NT + NM)
            rsqrt("mem", slice(32, 32 + NM), D, rstd[:, 32:32 + NM])
            for t in range(NM):
                dve.tensor_scalar(mem_tok[:, t, :], mem_tok[:, t, :], rstd[:, 32 + t:33 + t], None,
                                  ALU.mult).then_inc(xs_ready, 1)
            dve.wait_ge(dg_e, 1)
            link(dve.scalar_tensor_tensor(out=dg[:, 4, :], in0=dg[:, 0, :], scalar=0.0, in1=dg[:, 4, :],
                                          op0=ALU.max, op1=ALU.add))
            link(dve.tensor_scalar(dg[:, 4, :], dg[:, 4, :], -1.0, None, ALU.mult))
            link(dve.tensor_scalar(dg[:, 3, :], dg[:, 3, :], 1.0, None, ALU.add))
            tt(view(2), view(4), each(alog[:, :]), ALU.mult).then_inc(dg_g, 1)
            link(dve.reciprocal(dg[:, 3, :], dg[:, 3, :]))
            prep(after(("mq", 1)))
            for k in range(4):
                split_T(KD + k, ("cT", k), cT_hi[:, k, :], cT_lo[:, k, :], V_Q + k)
            for k in range(KD):
                split_T(KD + 4 + k, ("memT", k), memT_hi[:, k, :], memT_lo[:, k, :], V_MEM + k, MEM)
            for i in range(4):
                prep(after(("mkv", i)))

            def attention(name, nh, nk, pv_before):
                cols = nk * P
                width = 512 // nh

                def top(n):
                    filled(dve, (name, "S", n))
                    if n >= 4:
                        released(dve, (name, "S", n - 4))
                    dve.tensor_reduce(smax[:, n % 4:n % 4 + 1], bank((name, "S", n), P, cols), AX.X, ALU.max,
                                      negate=True).then_inc(max_ready, 1)

                def turned(n):
                    key = (name, "PT", n)
                    filled(dve, key)
                    if n >= 2:
                        if (n - 2) % nh == nh - 1:
                            filled(dve, (name, "O", (n - 2) // nh))
                        else:
                            dve.wait_ge(pv_done, pv_before + (n - 2) // nh * (nh - 1) + (n - 2) % nh + 1)
                    ins = dve.tensor_copy(pT[:, n % 2, 0:cols], bank(key, P, cols))
                    ins.then_inc(free(key), 1)

                def divide(t):
                    key = (name, "O", t)
                    filled(dve, key)
                    first = 0 if name == "mem" else NT
                    link(dve.reciprocal(rinv[:, t % 2, 0:nh], ssum[:, t % 2, 0:nh]))
                    if first + t > 0:
                        prev = (name, "oT", t - 1) if t else ("mem", "oT", NT - 1)
                        filled(dve, prev)
                    ins = tt(o_row[:, :].rearrange("p (h n) -> p h n", n=width),
                             bank(key).rearrange("p (h n) -> p h n", n=width), heads(rinv[:, t % 2, 0:nh], width), ALU.mult)
                    ins.then_inc(free(key), 1)

                top(0)
                for n in range(NT * nh):
                    if n + 1 < NT * nh:
                        top(n + 1)
                    turned(n)
                    if n % nh == 1 and n > nh:
                        divide(n // nh - 1)
                divide(NT - 1)

            filled(dve, ("gc",))
            ins = dve.tensor_copy(dg[:, 0, :], bank(("gc",), P, 64))
            ins.then_inc(free(("gc",)), 1)
            released(dve, ("gc",))
            filled(dve, ("gtot",))
            ins = dve.tensor_copy(dg[:, 1, :], bank(("gtot",), P, 64))
            ins.then_inc(free(("gtot",)), 1)
            released(dve, ("gtot",))
            link(dve.tensor_scalar(dg[:, 2, :], dg[:, 0, :], -1.0, None, ALU.mult))
            tt(dg[:, 5, :], dg[:, 1, :], dg[:, 0, :], ALU.subtract).then_inc(gc_ready, 1)
            attention("mem", MH, NM, 0)
            prep(("ukv", 0))
            prep(("z", 0))
            dve.wait_ge(kr_roped, 1)
            for t in range(NT):
                if t < 2:
                    filled(dve, ("qT", t + 2, 1))
                else:
                    filled(dve, ("kT", t - 2, 1))
                dst = qk_tok[:, t % 2, :].rearrange("p (h n) -> p h n", n=QK)
                for i, nm in enumerate(("kvA", "kvB")):
                    key = (nm, t)
                    dve.wait_ge(k_copied, 2 * t + i + 1)
                    dve.tensor_copy(dst[:, 4 * i:4 * i + 4, 0:NOPE],
                                    bank(key).rearrange("p (h n) -> p h n", n=128)[:, :, 0:NOPE]).then_inc(free(key), 1)
                kr = krab[:, t:t + 1, 0:ROPE].broadcast_to([P, H, ROPE])
                dve.tensor_copy(dst[:, :, NOPE:QK], kr).then_inc(k_placed, 1)
            attention("mla", H, NT, NT * (MH - 1))

            for t in range(NT):
                key = ("tok", t, 2)
                filled(dve, key)
                ins = dve.tensor_copy(v_tok[:, t, :], bank(key))
                ins.then_inc(free(key), 1)
                for pt in range(2):
                    n = 2 * t + pt
                    released(dve, ("tok", t, pt))
                    dve.tensor_reduce(small[:, 0, pt * 32 + t * 8:pt * 32 + t * 8 + 8],
                                      square2[:, n % 2, :].rearrange("p (h n) -> p h n", n=DK), AX.X,
                                      ALU.add).then_inc(sq_ready, 1)
            dve.wait_ge(sq_ready, 2 * NT)
            rsqrt("qk", slice(0, 64), 1.0, rstd[:, :])
            dve.tensor_scalar(rstd[:, 0:32], rstd[:, 0:32], DK ** -0.5, None, ALU.mult).then_inc(rstd_dn, 1)
            prep(after(("z", 0)))
            dve.wait_ge(gc_ready, 2)
            quantity = lambda q: rowq[:, :, 16 * q:16 * q + 16]
            link(dve.tensor_copy(quantity(0), view(0)))
            link(dve.tensor_scalar(quantity(1), view(3), -1.0, None, ALU.mult))
            link(dve.tensor_copy(quantity(3), view(4)))
            tt(quantity(2), quantity(1), quantity(3), ALU.mult).then_inc(rowq_ready, 1)
            dve.wait_ge(rows_hi_ready, 1)
            ins = tt(rows_rest[:, :, :], bank(("rows",), 64).rearrange("p (t n) -> p t n", t=NT), rows[0][:, :, :],
                     ALU.subtract)
            ins.then_inc(free(("rows",)), 1)
            released(dve, ("rows",))
            link(dve.tensor_copy(rows[1][:, :, :], rows_rest[:, :, :]))
            tt(rows[2][:, :, :], rows_rest[:, :, :], rows[1][:, :, :], ALU.subtract).then_inc(rows_ready, 1)
            for q in (1, 2, 3):
                dve.tensor_copy(pick[q][:, :, :, :].rearrange("p d j (u n) -> p (d j u) n", u=2),
                                ident_b[0:64, 16 * q:16 * q + 16].unsqueeze(2).broadcast_to([64, 16, 64])
                                ).then_inc(rows_ready, 1)
            released(dve, ("qkT", 7))

            def quad(key):
                return bank(key).rearrange("p (h n) -> p h n", h=4)

            def scan(g, step):
                for d in range(2):
                    n, t = 2 * g + d, tile_of(g, d)
                    if step == 0 and g > 0:
                        for which, dst, c0 in (("kg", kgT, 4), ("qg", qgT, 0)):
                            key = (which, g, d)
                            filled(dve, key)
                            if g > 1:
                                filled(dve, ("O", g - 1, d))
                            ins = tt(dst[:, d, :, :], dnT[:, c0:c0 + 4, t * P:(t + 1) * P], quad(key), ALU.mult)
                            ins.then_inc(free(key), 1)
                    if step == 1 and g > 0:
                        key = ("KS", g, d)
                        filled(dve, key)
                        dve.wait_ge(vb_ready, n + 1)
                        ins = tt(r_tok[:, d, :], r_tok[:, d, :], bank(key), ALU.add)
                        ins.then_inc(free(key), 1)
                    if step == 2 and g < NT - 1:
                        key = ("V", g, d)
                        filled(dve, key)
                        if g > 0:
                            filled(dve, ("KV", g - 1, d))
                        tt(vdec[:, d, :].rearrange("p (h n) -> p h n", n=DV), bank(key).rearrange("p (h n) -> p h n", n=DV),
                           heads(edec[:, col(t, d):col(t, d) + 8]), ALU.mult).then_inc(vdec_ready, 1)
                    if step == 3:
                        key = ("O", g, d)
                        if g >= 2:
                            filled(dve, key)
                            released(dve, ("O", NT - 1 - g, 1 - d))
                            ins = tt(o_tok[:, t, :], bank(key), o_tok[:, t, :], ALU.add)
                            ins.then_inc(free(key), 1)
                        if g < NT - 1:
                            key = ("KV", g, d)
                            filled(dve, key)
                            if g > 0:
                                dve.wait_ge(sg_ready, 2 * (g - 1) + d + 1)
                            for p in range(2):
                                h = slice(64 * p, 64 * p + 64)
                                src, dst = quad(key)[h, :, h], state[h, d, :, h]
                                if g == 0:
                                    ins = dve.tensor_copy(dst, src)
                                else:
                                    ins = tt(dst, src, state_g[h, d, :, h], ALU.add)
                            ins.then_inc(free(key), 1)

            dve.wait_ge(state_zero, 1)
            dve.wait_ge(consts_ready, 3)
            for g in range(NT):
                if g < NT:
                    for d in range(2):
                        t = tile_of(g, d)
                        key = ("kb", g, d)
                        filled(dve, key)
                        ins = tt(kbT[:, d, :, :], dnT[:, 4:8, t * P:(t + 1) * P], quad(key), ALU.mult)
                        ins.then_inc(free(key), 1)
                        for p in range(2):
                            b = 2 * d + p
                            released(dve, ("D", g, d, p))
                            key = ("G", g, d, p)
                            filled(dve, key)
                            ins = tt(NTm[:, b, :, :], decT[:, p, :, :], quad(key), ALU.mult)
                            ins.then_inc(free(key), 1)
                            key = ("A", g, d, p)
                            filled(dve, key)
                            ins = tt(attT[g % 2][:, b, :, :], decT[:, p, :, :], quad(key), ALU.mult)
                            ins.then_inc(free(key), 1)
                for s in range(1, LEVELS):
                    if g < NT:
                        for b in range(4):
                            key = ("P1", g, s, b)
                            filled(dve, key)
                            ins = tt(T1[:, b, :, :], quad(key), four(masks[:, 2 * s + b // 2, :]), ALU.mult)
                            ins.then_inc(free(key), 1)
                    if g > 0 and s <= 4:
                        scan(g - 1, s - 1)
            scan(NT - 1, 0)
            prep(("gate", 0, 0))
            for step in range(1, 4):
                scan(NT - 1, step)
            for d in range(2):
                filled(dve, ("O", NT - 1, d))
            prep(("gate", 0, 1))
            for t in range(NT):
                dve.wait_ge(o_squared, t + 1)
                dve.tensor_reduce(small[:, 0, t * 8:t * 8 + 8], square2[:, t % 2, :].rearrange("p (h n) -> p h n", n=DV),
                                  AX.X, ALU.add).then_inc(sq_ready, 1)
            prep(("gate", 0, 2))
            dve.wait_ge(sq_ready, 3 * NT)
            rsqrt("o", slice(0, 32), DV, rstd[:, 0:32])
            for t in range(NT):
                ov = o_tok[:, t, :].rearrange("p (h n) -> p h n", n=DV)
                tt(ov, ov, heads(rstd[:, t * 8:t * 8 + 8]), ALU.mult).then_inc(o_norm, 1)
            for b, src in ((0, oT_mla), (2, oT_mem)):
                dve.wait_ge(osplit_hi, 1 + b // 2)
                tt(oT_lo[:, b, :, :], src[:, :, :], f32(oT_hi[:, b, :, :]), ALU.subtract).then_inc(osplit_lo, 1)
            released(dve, ("z", 3))
            for k in range(4):
                key = ("odnT", k)
                filled(dve, key)
                by_row = lambda buf: buf[:, k, :].rearrange("p (c n) -> p n c", n=CHUNKS)
                ins = dve.scalar_tensor_tensor(out=by_row(oT_dn), in0=bank(key).rearrange("p (n c) -> p n c", n=CHUNKS),
                                               scalar=onorm[:, 0:1], in1=by_row(zT), op0=ALU.mult, op1=ALU.mult)
                ins.then_inc(free(key), 1)
            dve.wait_ge(osplit_hi, 3)
            tt(oT_lo[:, 1, :, :], oT_dn[:, :, :], f32(oT_hi[:, 1, :, :]), ALU.subtract).then_inc(osplit_lo, 1)
            for c in range(4):
                for b in range(3):
                    if c > 0 or b == 2:
                        prep(after(("gate", c, b)))
                for b in range(3):
                    prep(after(("br", c, b)))
                    for j in range(2):
                        key = ("br", c, b, j)
                        filled(dve, key)
                        released(dve, ("gate", c, b, j))
                        if b == 0:
                            if c > 0:
                                dve.wait_ge(merge_hi, 2 * (c - 1) + j + 1)
                            ins = tt(part[:, j, :], sig[:, j, :], bank(key), ALU.mult)
                            ins.then_inc(free(key), 1)
                        else:
                            if b == 1 and c > 0:
                                dve.wait_ge(merge_sum, 2 * (c - 1) + j + 1)
                            ins = tt(extra[:, j, :], sig[:, 2 * b + j, :], bank(key), ALU.mult)
                            ins.then_inc(free(key), 1)
                            released(dve, key)
                            ins = tt(part[:, j, :], part[:, j, :], extra[:, j, :], ALU.add)
                            if b == 2:
                                ins.then_inc(merge_sum, 1)
                            else:
                                link(ins)
                for j in range(2):
                    dve.wait_ge(merge_hi, 2 * c + j + 1)
                    tt(mT_lo[:, 2 * c + j, :], part[:, j, :], f32(mT_hi[:, 2 * c + j, :]), ALU.subtract).then_inc(merge_lo, 1)

            def residual(half, t):
                key = ("wo", half, t)
                filled(dve, key)
                xv = x1[:, t, 512 * half:512 * half + 512]
                ins = tt(xv, xv, bank(key), ALU.add)
                ins.then_inc(free(key), 1)

            for half in range(2):
                for kk in range(2):
                    prep(after(("wo", half, kk)))
                if half == 0:
                    dve.wait_ge(x1_landed, 16)
                for t in range(NT if half == 0 else 1):
                    residual(half, t)
            for t in range(NT):
                if t + 1 < NT:
                    residual(1, t + 1)
                dve.wait_ge(ssq_ready, NT + NM + t + 1)
                rsqrt("ffn", slice(t, t + 1), D, rstd[:, t:t + 1], t)
                dve.tensor_scalar(xs1[:, t, :], x1[:, t, :], rstd[:, t:t + 1], None, ALU.mult).then_inc(xs_ready, 1)
            for k in range(KD):
                split_T(2 * KD + 4 + k, ("h2T", k), hT_hi[:, k, :], hT_lo[:, k, :], V_FFN + k)
            for f in range(NF):
                prep(after(("gu", f)))
                key = ("u", f)
                filled(dve, key)
                released(dve, ("g", f))
                tt(bank(key), gate_act[:, f % 2, :], bank(key), ALU.mult).then_inc(glu_ready, 1)
                dve.wait_ge(glu_hi, f + 1)
                ins = tt(act_lo[:, f, :], bank(key), f32(act_hi[:, f, :]), ALU.subtract)
                ins.then_inc(free(key), 1)

            def add_glu(half, t):
                key = ("down", half, t)
                filled(dve, key)
                xv = x1[:, t, 512 * half:512 * half + 512]
                tt(xv, xv, bank(key), ALU.add).then_inc(x2_ready, 1)

            for half in range(2):
                for f0 in range(0, NF, 4):
                    prep(after(("down", half, f0)))
                for t in range(NT if half == 0 else 1):
                    add_glu(half, t)
            dve.wait_ge(fin_landed, 16)
            for t in range(NT):
                if t + 1 < NT:
                    add_glu(1, t + 1)
                dve.wait_ge(ssq_ready, 2 * NT + NM + t + 1)
                rsqrt("final", slice(t, t + 1), D, rstd[:, t:t + 1], t)
                dve.scalar_tensor_tensor(out=y_out[:, t, :], in0=x1[:, t, :], scalar=rstd[:, t:t + 1], in1=fin_w[:, :],
                                         op0=ALU.mult, op1=ALU.mult).then_inc(y_ready, 1)


_INS = ["x", "mem", "positions", "norm_mix", "w_in", "mla_q_norm", "mla_w_uq", "mla_kv_norm", "mla_w_ukv",
        "dn_conv", "dn_a_log", "dn_dt_bias", "dn_out_norm", "mem_norm", "mem_w_kv", "w_branch_mla",
        "w_branch_dn", "w_branch_mem", "w_out", "norm_ffn", "ffn_w_gate_up", "ffn_w_down", "final_norm"]


def kernel(**inputs):
    import numpy as _np
    import concourse.bacc as _bacc
    from concourse import mybir as _mybir
    from concourse.bass_utils import run_bass_kernel_spmd as _run

    nc = _bacc.Bacc("TRN2", target_bir_lowering=False, num_devices=1)
    arrays = {"in_tables_dram": shape_tables()}
    for name in _INS:
        arrays[f"in_{name}_dram"] = _np.ascontiguousarray(inputs[name])
    args = [nc.dram_tensor(n, a.shape, _mybir.dt.from_np(a.dtype), kind="ExternalInput").ap()
            for n, a in arrays.items()]
    out = nc.dram_tensor("out_0_dram", (1, SEQ, D), _mybir.dt.float32, kind="ExternalOutput").ap()
    hybrid_encoder_kernel(nc, *args, out)
    r = _run(nc, [arrays], core_ids=[0])
    return r.results[0]["out_0_dram"]
```
